# Optimizing a Trainium2 kernel written in Bass

```python
import math
import jax, jax.numpy as jnp
from jax import lax
import numpy as np

D_MODEL = 2048
BATCH = 1
SEQ = 256
DEPTH = 1

HEAD_DIM = 64
ATTN_WIDTH = D_MODEL // 2
N_Q_HEADS = ATTN_WIDTH // HEAD_DIM
N_KV_HEADS = N_Q_HEADS // 4
GQA_GROUP = N_Q_HEADS // N_KV_HEADS
N_BRANCH = 3
CMP_LEN = 32
CMP_STRIDE = 16
CMP_OVERLAP = CMP_LEN // CMP_STRIDE
SLC_LEN = 64
SLC_TOPK = 16
WINDOW = 512
Q_BLOCK = 64
CONV_CHANNELS = D_MODEL - ATTN_WIDTH
CONV_TAPS = 31
D_MIX = ATTN_WIDTH + CONV_CHANNELS
D_FF = ((8 * D_MODEL // 3 + 255) // 256) * 256
FFN_CONV_TAPS = 3
N_BUCKETS = 32
MAX_DISTANCE = 128
NORM_EPS = 1e-6
NEG_INF = -1e30

Q_COLS = ATTN_WIDTH
KV_COLS = N_BRANCH * 2 * N_KV_HEADS * HEAD_DIM
GATE_COLS = N_BRANCH * N_Q_HEADS
CONV_IN_COLS = 2 * CONV_CHANNELS
IN_COLS = Q_COLS + KV_COLS + GATE_COLS + CONV_IN_COLS


def rms_norm(x, g):
    xf = x.astype(jnp.float32)
    y = xf * lax.rsqrt(jnp.mean(xf * xf, axis=-1, keepdims=True) + NORM_EPS)
    return (y * g.astype(jnp.float32)).astype(x.dtype)

def layer_norm(x, g, b):
    xf = x.astype(jnp.float32)
    mu = jnp.mean(xf, axis=-1, keepdims=True)
    xc = xf - mu
    var = jnp.mean(xc * xc, axis=-1, keepdims=True)
    y = xc * lax.rsqrt(var + NORM_EPS) * g.astype(jnp.float32) + b.astype(jnp.float32)
    return y.astype(x.dtype)

def t5_bucket(dist):
    n = jnp.maximum(dist, 0)
    max_exact = N_BUCKETS // 2
    nf = jnp.maximum(n, 1).astype(jnp.float32)
    large = max_exact + (jnp.log(nf / max_exact) / math.log(MAX_DISTANCE / max_exact)
                         * (N_BUCKETS - max_exact)).astype(jnp.int32)
    large = jnp.minimum(large, N_BUCKETS - 1)
    return jnp.where(n < max_exact, n, large)

def masked_softmax(s, mask):
    s = jnp.where(mask, s.astype(jnp.float32), NEG_INF)
    p = jax.nn.softmax(s, axis=-1)
    return jnp.where(mask, p, 0.0)

def causal_depthwise_conv(x, w, b):
    taps, c = w.shape
    y = lax.conv_general_dilated(x, w[:, None, :].astype(x.dtype), window_strides=(1,),
                                 padding=[(taps - 1, 0)],
                                 dimension_numbers=('NWC', 'WIO', 'NWC'),
                                 feature_group_count=c)
    return y + b.astype(x.dtype)

def compress_tokens(tok, pos, w1, w2):
    b, t, h, d = tok.shape
    n_chunk = t // CMP_STRIDE
    n_cmp = n_chunk - CMP_OVERLAP + 1
    chunks = tok.reshape(b, n_chunk, CMP_STRIDE, h, d)
    blocks = jnp.concatenate([chunks[:, o:o + n_cmp] for o in range(CMP_OVERLAP)], axis=2)
    blocks = blocks + pos[None, None, :, None, :].astype(tok.dtype)
    flat = blocks.transpose(0, 1, 3, 2, 4).reshape(b, n_cmp, h, CMP_LEN * d)
    return jax.nn.silu(flat @ w1) @ w2

def nsa_attention(q, kv, gates, rel_bias, cmp_pos, cmp_w1, cmp_w2):
    b, t_len, hkv, g, dh = q.shape
    scale = HEAD_DIM ** -0.5
    k_cmp = compress_tokens(kv[:, :, 0, 0], cmp_pos[0], cmp_w1[0], cmp_w2[0])
    v_cmp = compress_tokens(kv[:, :, 0, 1], cmp_pos[1], cmp_w1[1], cmp_w2[1])
    n_cmp = k_cmp.shape[1]
    n_slc = t_len // SLC_LEN
    k_sel = min(SLC_TOPK, n_slc)
    k_slc = kv[:, :, 1, 0].reshape(b, n_slc, SLC_LEN, hkv, dh).transpose(0, 3, 1, 2, 4)
    v_slc = kv[:, :, 1, 1].reshape(b, n_slc, SLC_LEN, hkv, dh).transpose(0, 3, 1, 2, 4)
    pad = ((0, 0), (WINDOW, 0), (0, 0), (0, 0))
    k_win = jnp.pad(kv[:, :, 2, 0], pad)
    v_win = jnp.pad(kv[:, :, 2, 1], pad)
    ci_ = jnp.arange(n_cmp)[:, None]
    sj_ = jnp.arange(n_slc)[None, :]
    sel_map = ((ci_ * CMP_STRIDE < (sj_ + 1) * SLC_LEN) &
               (ci_ * CMP_STRIDE + CMP_LEN > sj_ * SLC_LEN)).astype(jnp.float32)
    cmp_end = jnp.arange(n_cmp, dtype=jnp.int32) * CMP_STRIDE + CMP_LEN - 1
    blk_ids = jnp.arange(n_slc, dtype=jnp.int32)[None, :]
    tab_t = rel_bias.reshape(N_BUCKETS, hkv, g).transpose(1, 0, 2)
    h_ar = jnp.arange(hkv)[None, :, None, None, None]
    gather_blocks = jax.vmap(jax.vmap(lambda blk, ii: blk[ii]))

    n_chunks = t_len // Q_BLOCK
    q_ch = q.reshape(b, n_chunks, Q_BLOCK, hkv, g, dh).transpose(1, 0, 3, 2, 4, 5)
    g_ch = gates.reshape(b, n_chunks, Q_BLOCK, hkv, g, N_BRANCH).transpose(1, 0, 3, 2, 4, 5)

    def chunk_fn(args):
        ci, qc, gc = args
        t = ci * Q_BLOCK + jnp.arange(Q_BLOCK, dtype=jnp.int32)
        qs = qc * scale
        s_cmp = jnp.einsum('bhqgd,bnhd->bhqgn', qs, k_cmp).astype(jnp.float32)
        bias_c = rel_bias[t5_bucket(t[:, None] - cmp_end[None, :])]
        bias_c = bias_c.reshape(Q_BLOCK, n_cmp, hkv, g).transpose(2, 0, 3, 1)
        valid_c = (cmp_end[None, :] <= t[:, None])[None, None, :, None, :]
        p_cmp = masked_softmax(s_cmp + bias_c.astype(jnp.float32), valid_c)
        o_cmp = jnp.einsum('bhqgn,bnhd->bhqgd', p_cmp.astype(v_cmp.dtype), v_cmp)
        imp = jnp.einsum('bhqgn,nj->bhqj', p_cmp, sel_map)
        cur = (t // SLC_LEN)[:, None]
        forced = (blk_ids == 0) | (blk_ids == cur) | (blk_ids == cur - 1)
        causal_blk = blk_ids * SLC_LEN <= t[:, None]
        imp = jnp.where(forced, jnp.inf, imp)
        imp = jnp.where(causal_blk, imp, -jnp.inf)
        _, idx = lax.top_k(imp, k_sel)
        kg = gather_blocks(k_slc, idx)
        vg = gather_blocks(v_slc, idx)
        pos = idx[..., None] * SLC_LEN + jnp.arange(SLC_LEN, dtype=jnp.int32)
        dist_s = t[None, None, :, None, None] - pos
        bias_s = jnp.moveaxis(tab_t[h_ar, t5_bucket(dist_s)], -1, 3)
        s_sel = jnp.einsum('bhqgd,bhqkld->bhqgkl', qs, kg).astype(jnp.float32)
        s_sel = (s_sel + bias_s.astype(jnp.float32)).reshape(b, hkv, Q_BLOCK, g, k_sel * SLC_LEN)
        valid_s = (dist_s >= 0).reshape(b, hkv, Q_BLOCK, 1, k_sel * SLC_LEN)
        p_sel = masked_softmax(s_sel, valid_s).reshape(b, hkv, Q_BLOCK, g, k_sel, SLC_LEN)
        o_sel = jnp.einsum('bhqgkl,bhqkld->bhqgd', p_sel.astype(vg.dtype), vg)
        kw = lax.dynamic_slice_in_dim(k_win, ci * Q_BLOCK, Q_BLOCK + WINDOW, axis=1)
        vw = lax.dynamic_slice_in_dim(v_win, ci * Q_BLOCK, Q_BLOCK + WINDOW, axis=1)
        kpos = ci * Q_BLOCK - WINDOW + jnp.arange(Q_BLOCK + WINDOW, dtype=jnp.int32)
        dist_w = t[:, None] - kpos[None, :]
        valid_w = ((dist_w >= 0) & (dist_w < WINDOW) & (kpos[None, :] >= 0))[None, None, :, None, :]
        bias_w = rel_bias[t5_bucket(dist_w)].reshape(Q_BLOCK, Q_BLOCK + WINDOW, hkv, g).transpose(2, 0, 3, 1)
        s_win = jnp.einsum('bhqgd,bshd->bhqgs', qs, kw).astype(jnp.float32)
        p_win = masked_softmax(s_win + bias_w.astype(jnp.float32), valid_w)
        o_win = jnp.einsum('bhqgs,bshd->bhqgd', p_win.astype(vw.dtype), vw)
        return gc[..., 0:1] * o_cmp + gc[..., 1:2] * o_sel + gc[..., 2:3] * o_win

    out = lax.map(chunk_fn, (jnp.arange(n_chunks, dtype=jnp.int32), q_ch, g_ch))
    out = out.transpose(1, 0, 3, 2, 4, 5)
    return out.reshape(b, t_len, ATTN_WIDTH)

def conformer_conv(h2, conv_w, conv_b, ln_g, ln_b):
    a, gate = jnp.split(h2, 2, axis=-1)
    u = a * jax.nn.sigmoid(gate)
    u = causal_depthwise_conv(u, conv_w, conv_b)
    u = layer_norm(u, ln_g, ln_b)
    return jax.nn.silu(u)

def conv_glu_ffn(h, w_up, cw, cb, w_down):
    u = causal_depthwise_conv(h @ w_up, cw, cb)
    a, gate = jnp.split(u, 2, axis=-1)
    return (jax.nn.silu(gate) * a) @ w_down

def first_inputs(seed: int = 0) -> dict:
    key = jax.random.key(seed)
    ks = jax.random.split(key, 18)
    f32 = jnp.float32
    nrm = lambda k, shape, s: jax.random.normal(k, shape, f32) * s
    return {
        "x": nrm(ks[0], (BATCH, SEQ, D_MODEL), 1.0),
        "rel_bias": nrm(ks[1], (N_BUCKETS, N_Q_HEADS), 0.5),
        "mix_norm_g": 1.0 + nrm(ks[2], (DEPTH, D_MODEL), 0.02),
        "w_in": nrm(ks[3], (DEPTH, D_MODEL, IN_COLS), D_MODEL ** -0.5),
        "cmp_pos": nrm(ks[4], (DEPTH, 2, CMP_LEN, HEAD_DIM), 0.1),
        "cmp_w1": nrm(ks[5], (DEPTH, 2, CMP_LEN * HEAD_DIM, HEAD_DIM), (CMP_LEN * HEAD_DIM) ** -0.5),
        "cmp_w2": nrm(ks[6], (DEPTH, 2, HEAD_DIM, HEAD_DIM), HEAD_DIM ** -0.5),
        "conv_w": nrm(ks[7], (DEPTH, CONV_TAPS, CONV_CHANNELS), CONV_TAPS ** -0.5),
        "conv_b": nrm(ks[8], (DEPTH, CONV_CHANNELS), 0.01),
        "conv_ln_g": 1.0 + nrm(ks[9], (DEPTH, CONV_CHANNELS), 0.02),
        "conv_ln_b": nrm(ks[10], (DEPTH, CONV_CHANNELS), 0.01),
        "w_out": nrm(ks[11], (DEPTH, D_MIX, D_MODEL), D_MIX ** -0.5),
        "ffn_norm_g": 1.0 + nrm(ks[12], (DEPTH, D_MODEL), 0.02),
        "w_up": nrm(ks[13], (DEPTH, D_MODEL, 2 * D_FF), D_MODEL ** -0.5),
        "ffn_conv_w": nrm(ks[14], (DEPTH, FFN_CONV_TAPS, 2 * D_FF), FFN_CONV_TAPS ** -0.5),
        "ffn_conv_b": nrm(ks[15], (DEPTH, 2 * D_FF), 0.01),
        "w_down": nrm(ks[16], (DEPTH, D_FF, D_MODEL), D_FF ** -0.5),
        "final_norm_g": 1.0 + nrm(ks[17], (D_MODEL,), 0.02),
    }

def first_block(x, rel_bias, mix_norm_g, w_in, cmp_pos, cmp_w1, cmp_w2, conv_w, conv_b,
              conv_ln_g, conv_ln_b, w_out, ffn_norm_g, w_up, ffn_conv_w, ffn_conv_b,
              w_down, final_norm_g):
    b, t_len, _ = x.shape
    splits = [Q_COLS, Q_COLS + KV_COLS, Q_COLS + KV_COLS + GATE_COLS]
    for l in range(DEPTH):
        h = rms_norm(x, mix_norm_g[l])
        proj = h @ w_in[l]
        q, kv, gate_logits, conv_in = jnp.split(proj, splits, axis=-1)
        q = q.reshape(b, t_len, N_KV_HEADS, GQA_GROUP, HEAD_DIM)
        kv = kv.reshape(b, t_len, N_BRANCH, 2, N_KV_HEADS, HEAD_DIM)
        gates = jax.nn.sigmoid(gate_logits).reshape(b, t_len, N_KV_HEADS, GQA_GROUP, N_BRANCH)
        attn = nsa_attention(q, kv, gates, rel_bias, cmp_pos[l], cmp_w1[l], cmp_w2[l])
        conv = conformer_conv(conv_in, conv_w[l], conv_b[l], conv_ln_g[l], conv_ln_b[l])
        x = x + jnp.concatenate([attn, conv], axis=-1) @ w_out[l]
        h = rms_norm(x, ffn_norm_g[l])
        x = x + conv_glu_ffn(h, w_up[l], ffn_conv_w[l], ffn_conv_b[l], w_down[l])
    return rms_norm(x, final_norm_g)


CHUNK = 64
Q_BLOCK_2 = 128
EPS = 1e-6
NEG_INF_2 = -1e30

MLA_HEADS = 16
MLA_Q_RANK = 768
MLA_KV_RANK = 512
MLA_NOPE = 128
MLA_ROPE = 64
MLA_V = 128
MLA_QK = MLA_NOPE + MLA_ROPE
ROPE_THETA = 10000.0

DIFF_HEADS = 8
DIFF_HEAD_DIM = 128
DIFF_V = 2 * DIFF_HEAD_DIM

N_BRANCH_2 = 2
MLA_MIX = MLA_HEADS * MLA_V
DIFF_MIX = DIFF_HEADS * DIFF_V

D_FF_2 = -(-8 * D_MODEL // (3 * 256)) * 256

IN_SIZES = (MLA_Q_RANK, MLA_KV_RANK, MLA_ROPE,
            DIFF_HEADS * 2 * DIFF_HEAD_DIM, DIFF_HEADS * 2 * DIFF_HEAD_DIM, DIFF_MIX,
            N_BRANCH_2 * D_MODEL)
D_IN = sum(IN_SIZES)


def rmsnorm(x, g):
    xf = x.astype(jnp.float32)
    y = xf * lax.rsqrt(jnp.mean(xf * xf, axis=-1, keepdims=True) + EPS)
    return (y * g.astype(jnp.float32)).astype(x.dtype)

def rope_tables(pos, dim):
    inv = ROPE_THETA ** (-jnp.arange(0, dim, 2, dtype=jnp.float32) / dim)
    ang = pos.astype(jnp.float32)[:, None] * inv[None, :]
    return jnp.cos(ang), jnp.sin(ang)

def apply_rope(x, cos, sin):
    half = x.shape[-1] // 2
    xf = x.astype(jnp.float32)
    x1, x2 = xf[..., :half], xf[..., half:]
    c, s = cos[:, None, :], sin[:, None, :]
    return jnp.concatenate([x1 * c - x2 * s, x2 * c + x1 * s], axis=-1).astype(x.dtype)

def to_blocks(a):
    b, s = a.shape[:2]
    return jnp.moveaxis(a.reshape((b, s // Q_BLOCK_2, Q_BLOCK_2) + a.shape[2:]), 1, 0)

def from_blocks(a):
    nb, b, q = a.shape[:3]
    return jnp.moveaxis(a, 0, 1).reshape((b, nb * q) + a.shape[3:])

def chunk_allowed(q_pos, k_pos):
    return (k_pos[None, :] // CHUNK) <= (q_pos[:, None] // CHUNK)

def mla_branch(c_q, c_kv, k_pe, q_norm_g, w_uq, kv_norm_g, w_ukv, cos, sin):
    b, s, _ = c_q.shape
    q = (rmsnorm(c_q, q_norm_g) @ w_uq).reshape(b, s, MLA_HEADS, MLA_QK)
    q_nope = q[..., :MLA_NOPE]
    q_rope = apply_rope(q[..., MLA_NOPE:], cos, sin)
    kv = (rmsnorm(c_kv, kv_norm_g) @ w_ukv).reshape(b, s, MLA_HEADS, MLA_NOPE + MLA_V)
    k_nope, v = kv[..., :MLA_NOPE], kv[..., MLA_NOPE:]
    k_rope = apply_rope(k_pe[:, :, None, :], cos, sin)[:, :, 0, :]
    k_pos = jnp.arange(s)
    scale = 1.0 / math.sqrt(MLA_QK)

    def blk(args):
        qn, qr, bi = args
        q_pos = bi * Q_BLOCK_2 + jnp.arange(Q_BLOCK_2)
        sc = (jnp.einsum('bqhd,bkhd->bhqk', qn, k_nope).astype(jnp.float32)
              + jnp.einsum('bqhr,bkr->bhqk', qr, k_rope).astype(jnp.float32)) * scale
        sc = jnp.where(chunk_allowed(q_pos, k_pos)[None, None], sc, NEG_INF_2)
        p = jax.nn.softmax(sc, axis=-1).astype(v.dtype)
        return jnp.einsum('bhqk,bkhd->bqhd', p, v)

    nb = s // Q_BLOCK_2
    o = lax.map(blk, (to_blocks(q_nope), to_blocks(q_rope), jnp.arange(nb)))
    return from_blocks(o).reshape(b, s, MLA_MIX)

def diff_branch(dq, dk, dv, lq1, lk1, lq2, lk2, sub_g, lambda_init, slopes):
    b, s, _ = dq.shape
    q = dq.reshape(b, s, DIFF_HEADS, 2, DIFF_HEAD_DIM)
    k = dk.reshape(b, s, DIFF_HEADS, 2, DIFF_HEAD_DIM)
    v = dv.reshape(b, s, DIFF_HEADS, DIFF_V)
    lam = (jnp.exp(jnp.sum(lq1.astype(jnp.float32) * lk1.astype(jnp.float32)))
           - jnp.exp(jnp.sum(lq2.astype(jnp.float32) * lk2.astype(jnp.float32)))
           + lambda_init)
    k_pos = jnp.arange(s)
    scale = 1.0 / math.sqrt(DIFF_HEAD_DIM)

    def blk(args):
        qb, bi = args
        q_pos = bi * Q_BLOCK_2 + jnp.arange(Q_BLOCK_2)
        dist = jnp.abs(q_pos[:, None] - k_pos[None, :]).astype(jnp.float32)
        alibi = -slopes[:, None, None] * dist[None]
        sc = jnp.einsum('bqhmd,bkhmd->bhmqk', qb, k).astype(jnp.float32) * scale
        sc = sc + alibi[None, :, None]
        sc = jnp.where(chunk_allowed(q_pos, k_pos)[None, None, None], sc, NEG_INF_2)
        p = jax.nn.softmax(sc, axis=-1)
        a = (p[:, :, 0] - lam * p[:, :, 1]).astype(v.dtype)
        return jnp.einsum('bhqk,bkhd->bqhd', a, v)

    nb = s // Q_BLOCK_2
    o = from_blocks(lax.map(blk, (to_blocks(q), jnp.arange(nb))))
    o = rmsnorm(o, sub_g) * (1.0 - lambda_init)
    return o.reshape(b, s, DIFF_MIX)

def second_inputs(seed: int = 0) -> dict:
    key = jax.random.key(seed)
    ks = jax.random.split(key, 24)

    def w(k, shape, fan_in):
        return jax.random.normal(k, shape, jnp.float32) * (fan_in ** -0.5)

    def gain(k, shape):
        return 1.0 + 0.02 * jax.random.normal(k, shape, jnp.float32)

    L = DEPTH
    return {
        "x": jax.random.normal(ks[0], (BATCH, SEQ, D_MODEL), jnp.float32),
        "attn_norm_g": gain(ks[1], (L, D_MODEL)),
        "w_in": w(ks[2], (L, D_MODEL, D_IN), D_MODEL),
        "b_gate": 0.01 * jax.random.normal(ks[3], (L, N_BRANCH_2 * D_MODEL), jnp.float32),
        "q_norm_g": gain(ks[4], (L, MLA_Q_RANK)),
        "w_uq": w(ks[5], (L, MLA_Q_RANK, MLA_HEADS * MLA_QK), MLA_Q_RANK),
        "kv_norm_g": gain(ks[6], (L, MLA_KV_RANK)),
        "w_ukv": w(ks[7], (L, MLA_KV_RANK, MLA_HEADS * (MLA_NOPE + MLA_V)), MLA_KV_RANK),
        "lambda_q1": 0.1 * jax.random.normal(ks[8], (L, DIFF_HEAD_DIM), jnp.float32),
        "lambda_k1": 0.1 * jax.random.normal(ks[9], (L, DIFF_HEAD_DIM), jnp.float32),
        "lambda_q2": 0.1 * jax.random.normal(ks[10], (L, DIFF_HEAD_DIM), jnp.float32),
        "lambda_k2": 0.1 * jax.random.normal(ks[11], (L, DIFF_HEAD_DIM), jnp.float32),
        "diff_norm_g": gain(ks[12], (L, DIFF_V)),
        "w_mla_proj": w(ks[13], (L, MLA_MIX, D_MODEL), MLA_MIX),
        "w_diff_proj": w(ks[14], (L, DIFF_MIX, D_MODEL), DIFF_MIX),
        "w_out": w(ks[15], (L, D_MODEL, D_MODEL), D_MODEL),
        "ffn_norm_g": gain(ks[16], (L, D_MODEL)),
        "w_ffn_gate": w(ks[17], (L, D_MODEL, D_FF_2), D_MODEL),
        "w_ffn_up": w(ks[18], (L, D_MODEL, D_FF_2), D_MODEL),
        "w_ffn_down": w(ks[19], (L, D_FF_2, D_MODEL), D_FF_2),
        "final_norm_g": gain(ks[20], (D_MODEL,)),
    }

def second_block(x, attn_norm_g, w_in, b_gate, q_norm_g, w_uq, kv_norm_g, w_ukv,
              lambda_q1, lambda_k1, lambda_q2, lambda_k2, diff_norm_g,
              w_mla_proj, w_diff_proj, w_out, ffn_norm_g, w_ffn_gate, w_ffn_up,
              w_ffn_down, final_norm_g):
    b, s, d = x.shape
    pos = jnp.arange(s)
    cos, sin = rope_tables(pos, MLA_ROPE)
    slopes = jnp.exp2(-8.0 * jnp.arange(1, DIFF_HEADS + 1, dtype=jnp.float32) / DIFF_HEADS)
    split_at = np.cumsum(IN_SIZES)[:-1].tolist()

    for i in range(DEPTH):
        lambda_init = 0.8 - 0.6 * math.exp(-0.3 * i)
        h = rmsnorm(x, attn_norm_g[i])
        proj = h @ w_in[i]
        c_q, c_kv, k_pe, dq, dk, dv, gate_logits = jnp.split(proj, split_at, axis=-1)

        y_mla = mla_branch(c_q, c_kv, k_pe, q_norm_g[i], w_uq[i], kv_norm_g[i], w_ukv[i], cos, sin)
        y_diff = diff_branch(dq, dk, dv, lambda_q1[i], lambda_k1[i], lambda_q2[i], lambda_k2[i],
                             diff_norm_g[i], lambda_init, slopes)

        g = jax.nn.sigmoid((gate_logits + b_gate[i]).astype(jnp.float32)).astype(x.dtype)
        g = g.reshape(b, s, N_BRANCH_2, d)
        merged = g[:, :, 0] * (y_mla @ w_mla_proj[i]) + g[:, :, 1] * (y_diff @ w_diff_proj[i])
        x = x + merged @ w_out[i]

        h2 = rmsnorm(x, ffn_norm_g[i])
        x = x + (jax.nn.silu(h2 @ w_ffn_gate[i]) * (h2 @ w_ffn_up[i])) @ w_ffn_down[i]

    return rmsnorm(x, final_norm_g)


def setup_inputs(seed=0):
    out = dict(first_inputs(seed))
    for name, value in second_inputs(seed + 1).items():
        if name != "x":
            out[name + "_2"] = value
    return out


def reference(
    x, rel_bias, mix_norm_g, w_in, cmp_pos, cmp_w1, cmp_w2, conv_w, conv_b, conv_ln_g,
    conv_ln_b, w_out, ffn_norm_g, w_up, ffn_conv_w, ffn_conv_b, w_down, final_norm_g,
    attn_norm_g_2, w_in_2, b_gate_2, q_norm_g_2, w_uq_2, kv_norm_g_2, w_ukv_2, lambda_q1_2,
    lambda_k1_2, lambda_q2_2, lambda_k2_2, diff_norm_g_2, w_mla_proj_2, w_diff_proj_2, w_out_2,
    ffn_norm_g_2, w_ffn_gate_2, w_ffn_up_2, w_ffn_down_2, final_norm_g_2,
):
    x = first_block(
        x, rel_bias, mix_norm_g, w_in, cmp_pos, cmp_w1, cmp_w2, conv_w, conv_b, conv_ln_g,
        conv_ln_b, w_out, ffn_norm_g, w_up, ffn_conv_w, ffn_conv_b, w_down, final_norm_g,
    )
    return second_block(
        x, attn_norm_g_2, w_in_2, b_gate_2, q_norm_g_2, w_uq_2, kv_norm_g_2, w_ukv_2,
        lambda_q1_2, lambda_k1_2, lambda_q2_2, lambda_k2_2, diff_norm_g_2, w_mla_proj_2,
        w_diff_proj_2, w_out_2, ffn_norm_g_2, w_ffn_gate_2, w_ffn_up_2, w_ffn_down_2,
        final_norm_g_2,
    )


_drawn_inputs = setup_inputs


def setup_inputs(seed=0):
    import zlib

    import numpy as np

    out = dict(_drawn_inputs(seed))
    spreads = {}
    factors = {'mix_norm_g': 3.949,
     'conv_b': 4.287,
     'conv_ln_g': 4.081,
     'conv_ln_b': 8.0,
     'ffn_norm_g': 3.248,
     'ffn_conv_b': 6.289,
     'attn_norm_g_2': 3.416,
     'b_gate_2': 21.687,
     'q_norm_g_2': 8.0,
     'kv_norm_g_2': 8.0,
     'lambda_k2_2': 4.734,
     'diff_norm_g_2': 24.047,
     'ffn_norm_g_2': 11.922,
     'final_norm_g_2': 21.855}
    for name, (base, spread) in spreads.items():
        noise = np.random.default_rng([zlib.crc32(name.encode()), seed]).standard_normal(out[name].shape)
        drawn = base * np.exp(spread * noise) if base else spread * noise
        out[name] = __import__('jax').numpy.asarray(drawn.astype(out[name].dtype))
    for name, factor in factors.items():
        out[name] = (out[name] * factor).astype(out[name].dtype)
    return out
```

```python
import math
from contextlib import ExitStack

import numpy as np
import concourse.bass as bass
from concourse import mybir

T = 256
D = 2048
P = 128
KT = D // P
QB = T // P
HD = 64
NQ, NKV = 16, 4
GRP = NQ // NKV
NBR = 3
CLEN, CSTR = 32, 16
NCMP = T // CSTR - 1
NCMP0 = (P - CLEN) // CSTR + 1
TAPS = 31
CCH = 1024
CT = CCH // P
KV0 = NQ * HD
GATE0 = KV0 + NBR * 2 * NKV * HD
CONV0 = GATE0 + NBR * NQ
NBKT, MAXD = 32, 128
DFF = 5632
FT = DFF // P
FTAPS = 3
EPS = 1e-6
NEG = -1e30
RQ, RKV = 768, 512
QT, KVT = RQ // P, RKV // P
MH, NOPE, ROPE = 16, 128, 64
MQK = NOPE + ROPE
KPE0 = RQ + RKV
DQ0 = KPE0 + ROPE
DH = 8
DK0, DV0, BG0 = DQ0 + D, DQ0 + 2 * D, DQ0 + 3 * D
MSCALE = 1.0 / math.sqrt(MQK)
DSCALE = 1.0 / math.sqrt(P)
LAM0 = 0.8 - 0.6 * math.exp(0.0)
CHUNK = 64
GC = 256
SLOT = 1152
R = 4
LEAD = 4
VEC = {}
_n = 0
for _name, _rows in (("mix_norm_g", 16), ("ffn_norm_g", 16), ("final_norm_g", 16), ("attn_norm_g_2", 16),
                     ("ffn_norm_g_2", 16), ("final_norm_g_2", 16), ("conv_b", 8), ("conv_ln_g", 8),
                     ("conv_ln_b", 8), ("q_norm_g_2", 6), ("kv_norm_g_2", 4), ("diff_norm_g_2", 2),
                     ("b_gate_2", 32), ("ffn_conv_b", 2 * FT), ("conv_w", TAPS * CT),
                     ("ffn_conv_w", FTAPS * 2 * FT), ("lambda_q1_2", 1), ("lambda_k1_2", 1),
                     ("lambda_q2_2", 1), ("lambda_k2_2", 1)):
    VEC[_name] = _n
    _n += _rows
NVEC = _n
VT = -(-NVEC // P)
CST = {}
_n = 0
for _name, _cols in (("ident", P), ("flip", P), ("rot", P), ("ones", P), ("cos", T), ("sin", T),
                     ("dist", 3 * P), ("mask", 3 * P), ("onehot", 3 * P), ("slope", DH), ("sees", 1)):
    CST[_name] = (_n, _n + _cols)
    _n += _cols
NCST = _n
PARTS = [(0, 16), (16, 16), (32, 12)]
PHASES = [("q", 8, 2, 4), ("kv", 8, 3, 4), ("gates", 2, 1, 1)]
PHASES += [(f"conv{g}", 4, GRP, 2) for g in range(2)]
PHASES += [("w_out", 8, 4, 4)]
for _p, (_t, _k) in enumerate(PARTS):
    PHASES += [(f"up1_{_p}", 8, _k // 2, 4), (f"down1_{_p}", 8, 4, 4)]
PHASES += [("latent", 8, 2, 4), ("latent_last", 4, 1, 2), ("kpe", 2, 1, 1), ("mla", 8, 8, 9), ("mla_proj", 8, 4, 4),
           ("diff", 16, 8, 8), ("diff_proj", 8, 4, 4), ("w_out_2", 8, 4, 4)]
for _p, (_t, _k) in enumerate(PARTS):
    PHASES += [(f"up2_{_p}", 8, _k // 2, 4), (f"down2_{_p}", 8, 4, 4)]
UPS, STEPS, CPS, U0, C0 = {}, {}, {}, {}, {}
_u = _c = 0
for _name, _us, _st, _cs in PHASES:
    UPS[_name], STEPS[_name], CPS[_name], U0[_name], C0[_name] = _us, _st, _cs, _u, _c
    _u += _us * _st
    _c += _cs * _st


VEC_LOADS = sum((VEC_END - 1) // P - r // P + 1 for r, VEC_END in zip(VEC.values(), [*list(VEC.values())[1:], NVEC]))
LINKS_A = {}
LINKS_V = dict.fromkeys(UPS, 0) | {"conv0": 25, "conv1": 25, "w_out": 4, "up1_0": 8, "down1_0": 4, "up1_1": 8, "down1_1": 4, "up1_2": 8, "down1_2": 4, "mla": 10, "mla_proj": 2, "diff": 15, "diff_proj": 5, "w_out_2": 4, "up2_0": 3, "down2_0": 4, "up2_1": 3, "down2_1": 4, "up2_2": 3, "down2_2": 4}
ROOT = {0: 1, "conv": 2, 1: 3, 2: 4, 3: 5, "latent": 6, "heads": 8, 4: 8 + DH, 5: 9 + DH}
NSPLIT = {0: 0, 1: 1, 3: 2, 4: 3}
NORM_GAIN = ("mix_norm_g", "ffn_norm_g", "final_norm_g", "attn_norm_g_2", "ffn_norm_g_2", "final_norm_g_2")
NSA_SEG = ((784, 784 + NCMP0), (512, 640), (640, 768), (768, 768 + NCMP), (0, 256), (256, 512))


def slot_of(ph, j):
    n = U0[ph] + j
    return n % R, n // R


def transfers(ph, j):
    return 4 if ph == "q" or (ph == "mla" and j < 2) else 2


RAW0, RAWS = {}, {}
_r = [0] * R
for _name, _us, _st, _cs in PHASES:
    RAW0[_name] = list(_r)
    RAWS[_name] = [sum(transfers(_name, _j) for _j in range(_us) if slot_of(_name, _j)[0] == _s) for _s in range(R)]
    _r = [a + _st * b for a, b in zip(_r, RAWS[_name])]


def arrived(ph, i, j):
    s = slot_of(ph, j)[0]
    before = sum(transfers(ph, k) for k in range(j + 1) if slot_of(ph, k)[0] == s)
    return i * (16 * RAWS[ph][s]) + 16 * (RAW0[ph][s] + before)


class Chain:

    def __init__(self, eng, sem):
        self.eng, self.sem, self.at, self.k, self.i, self.per = eng, sem, 0, 0, None, 0

    def link(self, ins):
        ins.then_inc(self.sem, 1)
        self.k += 1
        self.wait()

    def wait(self):
        at = self.at + self.k
        self.eng.wait_ge(self.sem, at if self.i is None else self.i * self.per + at)

    def wait_for(self, sem, value):
        self.eng.wait_ge(sem, value)

    def enter(self, i, per):
        self.at, self.k, self.i, self.per = self.at + self.k, 0, i, per

    def leave(self, steps, name=""):
        assert self.k == self.per, f"{name}: {self.k} links in a step, {self.per} declared"
        self.at, self.k, self.i = self.at + steps * self.per, 0, None


def constants():
    c = np.zeros((P, NCST), np.float32)

    def put(name, v):
        c[:v.shape[0], CST[name][0]:CST[name][0] + v.shape[1]] = v

    put("ident", np.eye(P))
    put("flip", np.eye(P)[::-1])
    rot = np.zeros((P, P))
    half = ROPE // 2
    for b in range(0, P, ROPE):
        for m in range(half):
            rot[b + m + half, b + m] = -1.0
            rot[b + m, b + m + half] = 1.0
    put("rot", rot)
    put("ones", np.ones((P, P)))
    inv = (np.float32(10000.0) ** (-np.arange(0, ROPE, 2, dtype=np.float32) / np.float32(ROPE))).astype(np.float32)
    ang = np.arange(T, dtype=np.float32)[None, :] * inv[:, None]
    put("cos", np.tile(np.cos(ang), (P // half, 1)))
    put("sin", np.tile(np.sin(ang), (P // half, 1)))
    q = np.arange(P)[:, None]
    dist, mask = [], []
    for b in range(QB):
        k = np.arange((b + 1) * P)[None, :]
        ok = k // CHUNK <= (q + b * P) // CHUNK
        dist.append(np.where(ok, np.abs(q + b * P - k), 1e33))
        mask.append(np.where(ok, 0.0, NEG))
    put("dist", np.concatenate(dist, 1))
    put("mask", np.concatenate(mask, 1))
    n = np.maximum(np.arange(T), 1).astype(np.float32)
    exact = NBKT // 2
    large = exact + (np.log(n / np.float32(exact)) / np.float32(math.log(MAXD / exact)) * np.float32(NBKT - exact)).astype(np.int32)
    bucket = np.where(np.arange(T) < exact, np.arange(T), np.minimum(large, NBKT - 1))
    hot = np.zeros((NBKT, 3 * P))
    hot[bucket[::-1], np.arange(T)] = 1.0
    put("onehot", hot)
    put("slope", np.tile(-np.exp2(-8.0 * np.arange(1, DH + 1) / DH)[None, :] / DSCALE, (P, 1)))
    put("sees", (np.arange(P)[:, None] >= CLEN - 1).astype(np.float32))
    return c


def program(nc, A, cst_d, out):
    f32, f32r = mybir.dt.float32, mybir.dt.float32r
    ACT, ALU = mybir.ActivationFunctionType, mybir.AluOpType
    X = mybir.AxisListType.X
    ds = bass.ds
    ctx = ExitStack()
    with ctx:
        def sb(name, shape, dt=f32):
            return ctx.enter_context(nc.sbuf_tensor(name, shape, dt))

        sems = {}

        def sem(name):
            if name not in sems:
                sems[name] = ctx.enter_context(nc.semaphore(name))
            return sems[name]

        w_raw = sb("w_raw", [P, R, SLOT])
        w_hi = sb("w_hi", [P, R, SLOT], f32r)
        w_lo = sb("w_lo", [P, R, SLOT], f32r)
        x = sb("x", [P, KT, T])
        hp = sb("hp", [P, KT, 2 * T], f32r)
        yp = sb("yp", [P, KT, 2 * T], f32r)
        cst = sb("cst", [P, NCST])
        vec = sb("vec", [P, VT * P])
        arena = sb("arena", [P, 15700])
        small = sb("small", [P, 64])
        banks = ctx.enter_context(nc.psum_tensor("banks", [P, 8, 512], f32))
        bias_d = nc.dram_tensor("bias_by_distance", (NQ, 3 * P), f32, kind="Internal").ap()

        def c_(name, rows=P, a=0, b=None):
            lo, hi = CST[name]
            return cst[0:rows, lo + a:hi if b is None else lo + b]

        ident, ones = c_("ident"), c_("ones")

        def area(at, *shape):
            n = int(np.prod(shape))
            v = arena[:, at:at + n]
            if len(shape) == 1:
                return v
            names = "abcde"[:len(shape)]
            return v.rearrange(f"p ({' '.join(names)}) -> p {' '.join(names)}", **dict(zip(names, shape)))

        W0, W1, Z, NV0 = 0, KT * T, 2 * KT * T, 15700 - 3 * T
        x_tok = area(W0, QB, D)
        vec_rows = area(Z, VT, P)
        nrm = area(W0, KT, T)
        sq = area(W1, KT, T)
        qT = area(W0, KT // 2, T)
        conv_y = area(W0 + KT // 2 * T, CT, T)
        w1k = area(W0 + KT // 2 * T, CLEN, HD)
        w1v = area(W1, CLEN, HD)
        biasT = area(W1, NQ, T)
        z = Z
        kvT = area(z, NBR, 2, 2, T); kvflat = area(z, 4 * NBR, T); z += 4 * NBR * T
        S = [area(z + 800 * a, 800) for a in range(2)]
        Xc = area(z, 2, 2 * CSTR, CSTR)
        bias_row = area(z + 1100, 3 * P)
        z += 1600
        vtm = area(z, 2, QB, 2, P); z += 8 * P
        vcm = area(z, 2, P); z += 2 * P
        kcm = area(z, 32); z += 32
        posT = area(z, 2, CLEN); z += 2 * CLEN
        gtok = area(z, QB, NBR * NQ); z += QB * NBR * NQ
        q_st = area(z, T)
        pos_rows = area(z, 2, 2, HD); z += T
        uc = area(z, T + 32); z += T + 32
        glu = area(z, 2, T)
        g_sb = area(z, T)
        w2 = area(z + T, 2, HD)
        hid = area(z + T + 2 * HD, 2, 2, 32)
        z += 2 * T
        assert z <= 15700, z
        ptA = [area(Z, 2 * T), area(Z + 6 * T, 2 * T)]
        ptB = [area(Z + 2 * T, 2 * T), area(Z + 10 * T, 2 * T)]
        merged = area(W0, KT, T)
        gate2 = area(W1, KT, T)
        lat = area(W0, QT + KVT, T)
        latsq = area(W1, QT + KVT, T)
        z = Z
        kpe = area(z, T); z += T
        kraw = area(z, T); z += T
        qn = area(z, 2, T); z += 2 * T
        qr = area(z, T); z += T
        qraw = area(z, T); z += T
        kn = area(z, 2, T); z += 2 * T
        vf = area(z, 2, T); z += 2 * T
        vt2 = area(z, 4, P); z += 4 * P
        gt = area(z, 2, T); z += 2 * T
        S2 = area(z, 2, 3 * P); z += 6 * P
        pt2 = area(z, 2, 3 * P); z += 6 * P
        dq, dk = qn, kn
        o_sb = area(z, 2, T); z += 2 * T
        o_sq = area(z, 2, T); z += 2 * T
        assert z <= NV0, z
        y_f = area(W1, KT, T)
        ua = area(W0, 2, T + 2)
        ug = area(W0 + 600, 2, T + 2)
        ca = area(W0 + 1200, 2, T)
        cg = area(W0 + 1800, 2, T)
        sg = area(W0 + 2400, 2, T)
        tmp = area(Z, 4, T)
        out_tok = area(Z, QB, D)
        nv = area(NV0, 3, T)

        def vcol(name, k=0, n=1):
            return vec[:, VEC[name] + k:VEC[name] + k + n]

        def vdyn(name, e):
            return vec[:, ds(e + VEC[name], 1)]

        def tile(t, e):
            return t[:, ds(e, 1), :].rearrange("p a b -> p (a b)")

        def pair(b):
            return banks[:, b, :].rearrange("p (a n) -> p n a", a=2)

        def rows(ap, kt0, n, cols):
            return ap[kt0 * P:(kt0 + n) * P].rearrange("(k p) n -> p k n", p=P)[:, :, cols]

        bias_win = yp[:, 0:KT // 2, :].bitcast(f32).rearrange("p k (a n) -> p (k a) n", a=2)

        block = ctx.enter_context(nc.Block())

        loaded = {n: sem("loaded_" + n) for n in ("x", "cst", "vec", "cmp", "bias_rows", "bias")}
        raw_ready = [sem(f"raw_ready{s}") for s in range(R)]
        lo_ready = [sem(f"lo_ready{s}") for s in range(R)]
        hi_ready = sem("hi_ready")
        unit_used = sem("unit_used")
        chunk_out = sem("chunk_out")
        steps_v, steps_a, steps_g = sem("vector_steps"), sem("scalar_steps"), sem("pool_steps")

        def all_lo(ph):
            return ph.startswith(("mla", "diff", "conv", "up1")) and not ph.endswith("proj") or UPS[ph] < 4

        def lo_by_vector(ph, j):
            return not all_lo(ph) and j % 4 == 3

        def unit_words(ph, j):
            if ph == "mla" and j < 2:
                return 3 * 384
            return 3 * GC if ph in ("down1_2", "down2_2") else 4 * GC

        FIRST = {n: m for (n, *_), (m, *_) in zip(PHASES, PHASES[1:])}

        @block.sync
        def _(sp):
            sp.dma_start(x_tok, A["x"][0].rearrange("(b p) d -> p b d", p=P)).then_inc(loaded["x"], 16)
            sp.dma_start(cst[:], cst_d).then_inc(loaded["cst"], 16)

            def unit(ph, i, j, parts):
                s, r = slot_of(ph, j)
                sp.wait_ge(lo_ready[s], i * (UPS[ph] // R) + (r + 1))
                for dst, src in parts:
                    sp.dma_start(dst(s), src).then_inc(raw_ready[s], 16)

            def view(k, n, a=0, b=None):
                return lambda s, k0=0, k1=None: w_raw[:, s, 0:k * n].rearrange("p (k n) -> p k n", n=n)[:, k0:k1, a:b]

            def halves(ph, i, j, w, kt0, k, col, n=GC):
                v = view(k, n)
                h = k // 2 if k > 1 else 1
                unit(ph, i, j, [(lambda s: v(s, 0, h), rows(w, kt0, h, ds(col, n))),
                                (lambda s: v(s, h, k), rows(w, kt0 + h, k - h, ds(col, n)))])

            def gemm(ph, w, k0, ktiles, col0):
                ku = ktiles // 4
                with sp.Fori(0, STEPS[ph]) as i:
                    for g in range(2):
                        col = sp.snap(i * (2 * GC) + (col0 + g * GC))
                        for u in range(4):
                            halves(ph, i, 4 * g + u, w, k0 + u * ku, ku, col)

            w_in = A["w_in"][0]
            with sp.Fori(0, STEPS["q"]) as i:
                for g in range(2):
                    for u in range(4):
                        cols = [sp.snap(i * (2 * GC) + (par * GC + g * P)) for par in range(2)]
                        unit("q", i, 4 * g + u, [(lambda s, par=par, c=c: w_raw[:, s, 0:4 * GC].rearrange(
                            "p (k c a d) -> p k c a d", k=4, c=2, a=2)[:, :, c, par, :],
                            rows(w_in, 4 * u, 4, ds(cols[par], P))[:, :, c * HD:(c + 1) * HD])
                            for par in range(2) for c in range(2)])
            gemm("kv", w_in, 0, KT, KV0)
            for u in range(2):
                halves("gates", 0, u, w_in, 8 * u, 8, GATE0, P)
            for pr in range(2):
                ph = f"conv{pr}"
                with sp.Fori(0, GRP) as i:
                    cols = [sp.snap(i * P + (CONV0 + half * CCH + pr * GRP * P)) for half in range(2)]
                    for u in range(4):
                        unit(ph, i, u, [(lambda s, h=h: w_raw[:, s, 0:4 * GC].rearrange(
                            "p (k n) -> p k n", n=GC)[:, :, h * P:(h + 1) * P],
                            rows(w_in, 4 * u, 4, ds(cols[h], P))) for h in range(2)])
            w_o = A["w_out"][0]
            with sp.Fori(0, 4) as i:
                for g in range(2):
                    col = sp.snap(i * (2 * GC) + g * GC)
                    for u in range(4):
                        if u < 2:
                            src = w_o[512 * u:512 * u + 512].rearrange("(a g d) n -> a d g n", a=2, g=GRP)
                            unit("w_out", i, 4 * g + u, [(lambda s, a=a: w_raw[a * HD:(a + 1) * HD, s, 0:4 * GC].rearrange(
                                "p (k n) -> p k n", n=GC), src[a][:, :, ds(col, GC)]) for a in range(2)])
                        else:
                            halves("w_out", i, 4 * g + u, w_o, 4 * u, 4, col)

            def ffn(blk, wa, ca0, wg, cg0, wd):
                for p, (t0, n) in enumerate(PARTS):
                    ph = f"up{blk}_{p}"
                    with sp.Fori(0, STEPS[ph]) as i:
                        for g, (w, c) in enumerate(((wa, ca0), (wg, cg0))):
                            col = sp.snap(i * GC + (c + t0 * P))
                            for u in range(4):
                                halves(ph, i, 4 * g + u, w, 4 * u, 4, col)
                    gemm(f"down{blk}_{p}", wd, t0, n, 0)

            ffn(1, A["w_up"][0], 0, A["w_up"][0], DFF, A["w_down"][0])
            w2_in = A["w_in_2"][0]
            gemm("latent", w2_in, 0, KT, 0)
            for u in range(4):
                halves("latent_last", 0, u, w2_in, 4 * u, 4, 4 * GC)
            for u in range(2):
                unit("kpe", 0, u, [(lambda s, h=h: w_raw[:, s, 0:8 * P].rearrange(
                    "p (k n) -> p k n", n=P)[:, :, h * ROPE:(h + 1) * ROPE],
                    rows(w2_in, 8 * u, 8, slice(KPE0, DQ0))) for h in range(2)])
            w_uq = A["w_uq_2"][0]
            with sp.Fori(0, STEPS["mla"]) as i:
                h0 = [sp.snap(i * (2 * MQK) + h * MQK) for h in range(2)]
                r0 = [sp.snap(i * (2 * MQK) + (h * MQK + NOPE)) for h in range(2)]
                ckv = [sp.snap(i * 512 + GC * u) for u in range(2)]
                cg = sp.snap(i * GC + BG0)
                for u in range(2):
                    src = w_uq[3 * u * P:(3 * u + 3) * P].rearrange("(k p) c -> p k c", p=P)
                    parts = []
                    for h in range(2):
                        parts.append((lambda s, h=h: view(3, 384, h * P, (h + 1) * P)(s), src[:, :, ds(h0[h], NOPE)]))
                        parts.append((lambda s, h=h: view(3, 384, 256 + h * ROPE, 256 + (h + 1) * ROPE)(s),
                                      src[:, :, ds(r0[h], ROPE)]))
                    unit("mla", i, u, parts)
                for u in range(2):
                    halves("mla", i, 2 + u, A["w_ukv_2"][0], 0, 4, ckv[u])
                for u in range(4):
                    halves("mla", i, 4 + u, w2_in, 4 * u, 4, cg)
            gemm("mla_proj", A["w_mla_proj_2"][0], 0, KT, 0)
            with sp.Fori(0, STEPS["diff"]) as i:
                cols = [sp.snap(i * GC + c) for c in (DQ0, DK0, DV0, BG0 + D)]
                for j, col in enumerate(cols):
                    for u in range(4):
                        halves("diff", i, 4 * j + u, w2_in, 4 * u, 4, col)
            gemm("diff_proj", A["w_diff_proj_2"][0], 0, KT, 0)
            gemm("w_out_2", A["w_out_2"][0], 0, KT, 0)
            ffn(2, A["w_ffn_up_2"][0], 0, A["w_ffn_gate_2"][0], 0, A["w_ffn_down_2"][0])
            for b in range(QB):
                sp.wait_ge(sem("out_ready"), 4 * (b + 1))
                sp.dma_start(out[0].rearrange("(b p) d -> p b d", p=P)[:, b, :], out_tok[:, b, :]).then_inc(sem("stored"), 16)
            sp.wait_ge(sem("stored"), 16 * QB)

        @block.scalar
        def _(act):
            at = Chain(act, steps_a)

            def link(ins):
                at.link(ins)

            act.dma_start(small[0:NBKT, 0:NQ], A["rel_bias"]).then_inc(loaded["bias_rows"], 16)

            def vec_load(name, ap):
                r, n, done = VEC[name], ap.shape[0], 0
                while done < n:
                    p, t = (r + done) % P, (r + done) // P
                    m = min(n - done, P - p)
                    act.dma_start(vec_rows[p:p + m, t, :], ap[done:done + m, :]).then_inc(loaded["vec"], 16)
                    vec_load.count += 1
                    done += m

            vec_load.count = 0
            for name in VEC:
                a = A[name]
                if len(a.shape) == 3:
                    a = a[0].rearrange("t (r c) -> (t r) c", c=P)
                else:
                    a = (a[0] if len(a.shape) == 2 else a).rearrange("(r c) -> r c", c=P)
                vec_load(name, a)
            assert vec_load.count == VEC_LOADS, vec_load.count

            def hi(ph, i, j):
                s, r = slot_of(ph, j)
                n = unit_words(ph, j)
                act.wait_ge(raw_ready[s], arrived(ph, i, j))
                act.wait_ge(unit_used, i * UPS[ph] + (U0[ph] + j + 1 - R + LEAD))
                nc.scalar.activation(w_hi[:, s, 0:n], w_raw[:, s, 0:n], ACT.Copy).then_inc(hi_ready, 1)

            def first(ph):
                for j in range(min(4, UPS[ph])):
                    hi(ph, 0, j)

            def stream(ph, mid=None, post=None, split=None, pre_next=True):
                def step(i, last):
                    for j in range(4, UPS[ph]):
                        if j == split:
                            mid(i)
                        hi(ph, i, j)
                    if mid and split is None:
                        mid(i)
                    if not last:
                        for j in range(4):
                            hi(ph, i + 1, j)
                    elif pre_next:
                        first(FIRST[ph])
                    if post:
                        post(i)

                with act.Fori(0, STEPS[ph] - 1) as i:
                    per = LINKS_A.get(ph, 0)
                    at.enter(i, per)
                    step(i, False)
                at.leave(STEPS[ph] - 1, ph)
                step(STEPS[ph] - 1, True)

            def norm(k):
                if k in (0, 3):
                    for b in range(KT // 2):
                        if k == 0:
                            act.wait_ge(sem("x_transposed"), b + 1)
                        else:
                            act.wait_ge(sem("x_normed"), b // 2 + 1)
                        nc.scalar.activation(sq[:, 2 * b:2 * b + 2, :], x[:, 2 * b:2 * b + 2, :], ACT.Square)\
                            .then_inc(sem("squares"), 1)
                root(ROOT[k])
                for b in range(4):
                    act.wait_ge(sem("normed"), 4 * NSPLIT[k] + b + 1)
                    nc.scalar.activation(hp[:, 4 * b:4 * b + 4, 0:T], nrm[:, 4 * b:4 * b + 4, :], ACT.Copy)\
                        .then_inc(sem("normed_hi"), 1)

            def root(count):
                act.wait_ge(sem("variance"), count)
                nc.scalar.activation(nv[:, 1, :], nv[:, 0, :], ACT.Sqrt).then_inc(sem("rooted"), 1)

            def squares(ph):
                def run(i):
                    for g in range(2):
                        act.wait_ge(chunk_out, i * 4 + (C0[ph] + 2 * g + 2 + LEAD))
                        t = ds(i * 4 + 2 * g, 2)
                        nc.scalar.activation(sq[:, t, :], x[:, t, :], ACT.Square).then_inc(sem("squares"), 1)
                return run

            first("q")
            norm(0)
            act.wait_ge(sem("normed_lo"), 4)
            for half in range(2):
                lo, hi_ = half * HD, (half + 1) * HD
                for kv, w1 in enumerate((w1k, w1v)):
                    act.dma_start(w1[lo:hi_], A["cmp_w1"][0, kv].rearrange("(l d) j -> d l j", d=HD)).then_inc(loaded["cmp"], 16)
                    act.dma_start(pos_rows[0:CLEN, kv, half, :], A["cmp_pos"][0, kv]).then_inc(loaded["cmp"], 16)
                    act.dma_start(w2[lo:hi_, kv, :], A["cmp_w2"][0, kv]).then_inc(loaded["cmp"], 16)
            stream("q")
            stream("kv", pre_next=True)
            first("conv0")
            act.wait_ge(sem("gates_tok"), 1)
            nc.scalar.activation(gtok, gtok, ACT.Exp, scale=-1.0).then_inc(sem("gates_exp"), 1)
            act.wait_ge(sem("hidden"), 1)
            nc.scalar.activation(hid[:, 1, :, 0:2 * NCMP], hid[:, 0, :, 0:2 * NCMP], ACT.Exp, scale=-1.0).then_inc(sem("hidden_exp"), 1)

            def nsa(pr):
                ph = f"conv{pr}"

                def step(i, last):
                    n = pr * GRP
                    for a in range(2):
                        act.wait_ge(sem("nsa_max"), 2 * i + (2 * n + a + 1))
                        e, l = S[a], small[:, 32 + 8 * a:38 + 8 * a]
                        m = small[:, 16 + 8 * a:22 + 8 * a]
                        for j, (lo, hi_) in enumerate(NSA_SEG):
                            ins = nc.scalar.activation(e[:, lo:hi_], e[:, lo:hi_], ACT.Exp, bias=m[:, j:j + 1],
                                                       accum_out=l[:, j:j + 1])
                        ins.then_inc(sem("nsa_exp"), 1)
                    for a in range(2):
                        act.wait_ge(sem("nsa_coef"), 2 * i + (2 * n + a + 1))
                        c = small[:, 48 + 6 * a:54 + 6 * a]
                        for j, (lo, hi_) in enumerate(NSA_SEG):
                            ins = nc.scalar.activation(S[a][:, lo:hi_], S[a][:, lo:hi_], ACT.Copy, scale=c[:, j:j + 1])
                        ins.then_inc(sem("nsa_p"), 1)

                    def next_units(j0, j1):
                        for j in range(j0, j1):
                            if not last:
                                hi(ph, i + 1, j)
                            else:
                                hi(FIRST[ph], 0, j)

                    next_units(0, 2)
                    for a in range(2):
                        act.wait_ge(sem("nsa_turned"), 2 * i + (2 * n + a + 1))
                        nc.scalar.activation(ptA[a], banks[:, 4 + 2 * a, :], ACT.Copy)
                        nc.scalar.activation(ptB[a][:, 0:256], banks[:, 5 + 2 * a, 0:256], ACT.Copy)
                        nc.scalar.activation(ptB[a][0:NCMP, 256:512], banks[0:NCMP, 5 + 2 * a, 256:512], ACT.Copy)\
                            .then_inc(sem("nsa_pt"), 1)
                    if not (last and pr == 1):
                        scaled(i + (n + 1))
                    next_units(2, 4)
                    act.wait_ge(chunk_out, i * 2 + (C0[ph] + 2 + LEAD))
                    nc.scalar.activation(glu[:, 1, :], glu[:, 1, :], ACT.Exp, scale=-1.0).then_inc(sem("glu_exp"), 1)

                with act.Fori(0, GRP - 1) as i:
                    step(i, False)
                step(GRP - 1, True)

            def scaled(e):
                if not isinstance(e, int):
                    act.wait_ge(sem("nsa_turned"), 2 * e)
                nc.scalar.activation(q_st, tile(qT, e), ACT.Copy, scale=HD ** -0.5).then_inc(sem("nsa_q"), 1)

            scaled(0)
            nsa(0)
            nsa(1)
            act.wait_ge(sem("conv_centred"), 1)
            nc.scalar.activation(sq[:, 0:CT, :], conv_y, ACT.Square).then_inc(sem("conv_squares"), 1)
            root(ROOT["conv"])
            act.wait_ge(sem("conv_affine"), 1)
            nc.scalar.activation(sq[:, 0:CT, :], conv_y, ACT.Sigmoid).then_inc(sem("conv_sigmoid"), 1)
            act.wait_ge(sem("conv_gated"), 1)
            nc.scalar.activation(yp[:, CT:KT, 0:T], conv_y, ACT.Copy).then_inc(sem("conv_hi"), 1)
            stream("w_out", post=squares("w_out"))
            norm(1)

            def ffn(blk):
                for p, (t0, n) in enumerate(PARTS):
                    up = f"up{blk}_{p}"
                    done = (blk - 1) * FT // 2 + t0 // 2

                    def gate(i):
                        act.wait_ge(sem("ffn_gate"), i + (done + 1))
                        nc.scalar.activation(sg, cg, ACT.Sigmoid).then_inc(sem("ffn_sigmoid"), 1)

                    stream(up, post=gate)
                    down = f"down{blk}_{p}"
                    stream(down, post=squares(down) if p == 2 else None, pre_next=not (blk == 2 and p == 2))

            ffn(1)
            root(ROOT[2])
            norm(3)
            stream("latent")
            first("kpe")
            for k, (a, b) in enumerate(((0, QT), (QT, QT + KVT))):
                act.wait_ge(chunk_out, C0["latent"] + b + LEAD)
                nc.scalar.activation(latsq[:, a:b, :], lat[:, a:b, :], ACT.Square).then_inc(sem("latent_squares"), 1)
                root(ROOT["latent"] + k)
            act.wait_ge(sem("lambda_sums"), 1)
            nc.scalar.activation(small[:, 4:6], small[:, 2:4], ACT.Exp).then_inc(sem("lambda_exp"), 1)
            first("mla")

            def gate_exp(ph, k0):
                def run(i):
                    act.wait_ge(chunk_out, i * CPS[ph] + (C0[ph] + CPS[ph] + LEAD))
                    for c in range(2):
                        ins = nc.scalar.activation(gt[:, c, :], gt[:, c, :], ACT.Exp, bias=vdyn("b_gate_2", i * 2 + (k0 + c)), scale=-1.0)
                    ins.then_inc(sem("bgate_exp"), 1)
                return run

            def soft2(name, scale):
                def run(i):
                    for a in range(2):
                        act.wait_ge(sem(name + "_max"), 2 * i + (a + 1))
                        for b in range(QB):
                            lo, hi_ = (0, P) if b == 0 else (P, 3 * P)
                            ins = nc.scalar.activation(S2[:, a, lo:hi_], S2[:, a, lo:hi_], ACT.Exp,
                                                       bias=small[:, 16 + 2 * a + b:17 + 2 * a + b], scale=scale,
                                                       accum_out=small[:, 24 + 2 * a + b:25 + 2 * a + b])
                        ins.then_inc(sem(name + "_exp"), 1)
                return run

            stream("mla", mid=soft2("mla", MSCALE), post=gate_exp("mla", 0))
            for b in range(4):
                act.wait_ge(sem("mla_out"), STEPS["mla"])
                nc.scalar.activation(yp[:, 4 * b:4 * b + 4, 0:T], y_f[:, 4 * b:4 * b + 4, :], ACT.Copy)\
                    .then_inc(sem("mla_hi"), 1)
            stream("mla_proj")

            def diff_post(i):
                gate_exp("diff", KT)(i)
                act.wait_ge(sem("o_out"), i + 1)
                nc.scalar.activation(o_sq, o_sb, ACT.Square).then_inc(sem("o_squares"), 1)
                root(i + ROOT["heads"])

            stream("diff", mid=soft2("diff", DSCALE), split=12, post=diff_post)
            stream("diff_proj")
            stream("w_out_2", post=squares("w_out_2"))
            norm(4)
            ffn(2)
            root(ROOT[5])

        @block.gpsimd
        def _(pool):
            for s in range(R):
                nc.gpsimd.memset(small[:, 60 + s:61 + s], 0.0).then_inc(lo_ready[s], 1)

            pool.wait_ge(sem("bias_row"), 1)
            pool.dma_start(bias_d, bias_row[0:NQ, :]).then_inc(sem("bias_stored"), 16)
            pool.wait_ge(sem("bias_stored"), 16)
            pool.dma_start(bias_win, bass.AP(bias_d.tensor, 0, [[1, P], [3 * P, NQ], [1, T]])).then_inc(loaded["bias"], 16)

            def lo(ph, i, j):
                s, r = slot_of(ph, j)
                n = unit_words(ph, j)
                pool.wait_ge(hi_ready, i * UPS[ph] + (U0[ph] + j + 1))
                nc.gpsimd.tensor_tensor(w_lo[:, s, 0:n], w_raw[:, s, 0:n], w_hi[:, s, 0:n].bitcast(f32),
                                        ALU.subtract).then_inc(lo_ready[s], 1)

            def lows(ph):
                js = [j for j in range(UPS[ph]) if not lo_by_vector(ph, j)]
                if STEPS[ph] == 1:
                    for j in js:
                        lo(ph, 0, j)
                    return
                with pool.Fori(0, STEPS[ph]) as i:
                    for j in js:
                        lo(ph, i, j)

            for ph, *_ in PHASES:
                lows(ph)

        @block.vector
        def _(dve):
            v = nc.vector
            at = Chain(dve, steps_v)
            link = at.link

            def lo(ph, i, j):
                s, r = slot_of(ph, j)
                n = unit_words(ph, j)
                dve.wait_ge(hi_ready, i * UPS[ph] + (U0[ph] + j + 1))
                v.tensor_tensor(w_lo[:, s, 0:n], w_raw[:, s, 0:n], w_hi[:, s, 0:n].bitcast(f32), ALU.subtract)\
                    .then_inc(lo_ready[s], 1)

            def first(ph):
                if UPS[ph] >= 4 and lo_by_vector(ph, 3):
                    lo(ph, 0, 3)

            def used(ph, i, j):
                dve.wait_ge(unit_used, i * UPS[ph] + (U0[ph] + j + LEAD))

            def take(dst, b, rows=P):
                v.tensor_reduce(dst, pair(b)[0:rows], X, ALU.add).then_inc(chunk_out, 1)

            def loop(ph, step, n0=0):
                with dve.Fori(n0, STEPS[ph] - 1) as i:
                    at.enter(i - n0 if n0 else i, LINKS_V[ph])
                    step(i, False)
                at.leave(STEPS[ph] - 1 - n0, ph)
                step(STEPS[ph] - 1, True)

            def stream(ph, out_a, out_b, work=None, pre_next=True):
                def step(i, last):
                    if lo_by_vector(ph, 7):
                        lo(ph, i, 7)
                    used(ph, i, 4)
                    out_a(i)
                    if not last:
                        if lo_by_vector(ph, 3):
                            lo(ph, i + 1, 3)
                    elif pre_next:
                        first(FIRST[ph])
                    used(ph, i, 8)
                    out_b(i)
                    if work:
                        work(i)
                loop(ph, step)

            def root_of(src, n, count):
                v.tensor_scalar(nv[:, 0, :], src, 1.0 / n, EPS, ALU.mult, ALU.add).then_inc(sem("variance"), 1)
                dve.wait_ge(sem("rooted"), count)
                link(v.reciprocal(nv[:, 2, :], nv[:, 1, :]))
                link(v.tensor_tensor(nv[:, 1, :], nv[:, 2, :], nv[:, 2, :], ALU.mult))
                link(v.scalar_tensor_tensor(nv[:, 1, :], nv[:, 1, :], -0.5, nv[:, 0, :], ALU.mult, ALU.mult))
                link(v.scalar_tensor_tensor(nv[:, 2, :], nv[:, 1, :], 1.5, nv[:, 2, :], ALU.add, ALU.mult))

            def norm(k):
                dve.wait_ge(sem("sum_of_squares"), k + 1)
                root_of(banks[:, 4, 0:T], D, ROOT[k])
                dst = x if k == 2 else nrm
                done = {2: "x_normed", 5: "final_normed"}.get(k, "normed")

                def scale(b):
                    for t in range(4 * b, 4 * b + 4):
                        ins = v.scalar_tensor_tensor(dst[:, t, :], x[:, t, :], vcol(NORM_GAIN[k], t), nv[:, 2, :], ALU.mult, ALU.mult)
                    ins.then_inc(sem(done), 1)

                def low(b):
                    dve.wait_ge(sem("normed_hi"), 4 * NSPLIT[k] + b + 1)
                    v.tensor_tensor(hp[:, 4 * b:4 * b + 4, T:], nrm[:, 4 * b:4 * b + 4, :],
                                    hp[:, 4 * b:4 * b + 4, 0:T].bitcast(f32), ALU.subtract).then_inc(sem("normed_lo"), 1)

                for b in range(4):
                    scale(b)
                    if b and k in NSPLIT:
                        low(b - 1)
                if k in NSPLIT:
                    low(3)

            v.memset(small[:, 59:60], 0.0).then_inc(chunk_out, LEAD)
            dve.wait_ge(sem("bias_mm"), 1)
            v.memset(bias_row[0:NQ, T:], NEG)
            v.tensor_copy(bias_row[0:NQ, 0:T], banks[0:NQ, 7, 0:T]).then_inc(sem("bias_row"), 1)
            for k in range(8):
                dve.wait_ge(sem("x_turned"), k + 1)
                v.tensor_copy(x[:, 2 * k:2 * k + 2, :], banks[:, k, :].rearrange("p (a n) -> p a n", a=2))\
                    .then_inc(sem("x_transposed"), 1)
            dve.wait_ge(sem("vec_turned"), 1)
            v.tensor_copy(vec[:, 0:512], banks[:, 0, :])
            link(v.tensor_copy(vec[:, 512:VT * P], banks[:, 1, 0:VT * P - 512]))
            v.tensor_scalar(vcol("b_gate_2", 0, 32), vcol("b_gate_2", 0, 32), -1.0, None, ALU.mult)
            v.tensor_scalar(vcol("diff_norm_g_2", 0, 2), vcol("diff_norm_g_2", 0, 2), 1.0 - LAM0, None, ALU.mult)
            v.tensor_tensor(small[:, 8:9], vcol("lambda_q1_2"), vcol("lambda_k1_2"), ALU.mult)
            link(v.tensor_tensor(small[:, 9:10], vcol("lambda_q2_2"), vcol("lambda_k2_2"), ALU.mult))
            first("q")
            norm(0)

            def to(dst, c0):
                def run(i):
                    for c in range(2):
                        take(tile(dst, i * 4 + (c0 + c)), c0 + c)
                return run

            stream("q", to(qT, 0), to(qT, 2))
            stream("kv", to(kvflat, 0), to(kvflat, 2))
            used("gates", 0, 2)
            take(g_sb[0:NBR * NQ, :], 0, NBR * NQ)
            dve.wait_ge(sem("gates_turned"), 1)
            v.tensor_copy(gtok, banks[:, 4, 0:QB * NBR * NQ].rearrange("p (b n) -> p b n", b=QB)).then_inc(sem("gates_tok"), 1)
            dve.wait_ge(sem("gates_exp"), 1)
            link(v.tensor_scalar(gtok, gtok, 1.0, None, ALU.add))
            link(v.reciprocal(gtok, gtok))
            g0 = gtok[:, 0, :].rearrange("p (h r) -> p h r", r=NBR)[:, :, 0]
            link(v.tensor_scalar(g0, g0, c_("sees"), None, ALU.mult))
            dve.wait_ge(sem("pos_turned"), 1)
            link(v.tensor_copy(posT, banks[:, 5, 0:2 * CLEN].rearrange("p (a n) -> p a n", a=2)))
            dve.wait_ge(loaded["bias"], 16)
            for kv in range(2):
                if kv:
                    dve.wait_ge(sem("hidden_mm"), 1)
                src = kvT[:, 0, kv].rearrange("p a (n r) -> p (a n) r", r=CSTR)
                for o in range(2):
                    ins = v.tensor_tensor(Xc[:, o], src, posT[:, kv, o * CSTR:(o + 1) * CSTR].unsqueeze(1)
                                          .to_broadcast([P, 2 * CSTR, CSTR]), ALU.add)
                ins.then_inc(sem("blocks"), 1)
            for br in range(2):
                dve.wait_ge(sem("v_turned"), br + 1)
                v.tensor_copy(vtm[:, br], banks[:, 7 if br == 0 else 4, :].rearrange("p (k a n) -> p k a n", k=QB, a=2))\
                    .then_inc(sem("v_tok"), 1)
            dve.wait_ge(sem("hidden_mm"), 2)
            hv, he = hid[:, 0, :, 0:2 * NCMP], hid[:, 1, :, 0:2 * NCMP]
            v.tensor_copy(hv, banks[:, 6, 0:64].rearrange("p (a n) -> p a n", a=2)[:, :, 0:2 * NCMP]).then_inc(sem("hidden"), 1)
            dve.wait_ge(sem("hidden_exp"), 1)
            link(v.tensor_scalar(he, he, 1.0, None, ALU.add))
            link(v.reciprocal(he, he))
            v.tensor_tensor(hv, hv, he, ALU.mult).then_inc(sem("hidden_act"), 1)
            dve.wait_ge(sem("cmp_mm"), 1)
            v.tensor_copy(kcm[:, 0:2 * NCMP], banks[:, 5, 128:128 + 2 * NCMP])
            for a in range(2):
                ins = v.tensor_copy(vcm[0:NCMP, :, a * HD:(a + 1) * HD],
                                    banks[0:NCMP, 5 + a, 256:256 + 2 * HD].rearrange("p (a n) -> p a n", a=2))
            ins.then_inc(sem("cmp_kv"), 1)
            for k in range(8):
                dve.wait_ge(sem("bias_flipped"), k + 1)
                v.tensor_copy(biasT[:, 2 * k:2 * k + 2, :], banks[:, 6 + k % 2, :].rearrange("p (a n) -> p a n", a=2))\
                    .then_inc(sem("bias_ready"), 1)
            link(v.memset(uc[:, 0:32], 0.0))
            v.memset(small[:, 7:8], 0.0).then_inc(sem("nsa_out"), 1)

            def bcast(ap, n):
                return ap.unsqueeze(1).to_broadcast([P, n, ap.shape[-1]])

            def nsa(pr):
                ph, n = f"conv{pr}", pr * GRP

                def step(i, last, before=True):
                    for a in range(2):
                        e, m = S[a], small[:, 16 + 8 * a:22 + 8 * a]
                        late, early = banks[:, 4 + 2 * a, :], banks[:, 5 + 2 * a, :]
                        bt = tile(biasT, i + (2 * n + GRP * a))
                        dve.wait_ge(sem("nsa_scores"), 2 * i + (2 * n + a + 1))
                        two = lambda ap: ap.rearrange("p (a n) -> p a n", a=2)
                        v.tensor_tensor(two(e[:, 0:512]), two(late), bcast(bt, 2), ALU.add)
                        v.tensor_tensor(two(e[:, 512:768]), two(early[:, 0:256]), bcast(bt[:, P:T], 2), ALU.add)
                        v.tensor_tensor(e[:, 768:768 + NCMP], early[:, 256:256 + NCMP], bt[:, CLEN - 1::CSTR], ALU.add)
                        link(v.tensor_tensor(e[:, 784:784 + NCMP0], early[:, 272:272 + NCMP0],
                                             bt[:, P + CLEN - 1:P + CLEN - 1 + CSTR * (NCMP0 - 1) + 1:CSTR], ALU.add))
                        v.tensor_reduce(m[:, 4:6], two(e[:, 0:512]), X, ALU.max, negate=True)
                        v.tensor_reduce(m[:, 1:3], two(e[:, 512:768]), X, ALU.max, negate=True)
                        v.tensor_reduce(m[:, 3:4], e[:, 768:768 + NCMP], X, ALU.max, negate=True)
                        v.tensor_reduce(m[:, 0:1], e[:, 784:784 + NCMP0], X, ALU.max, negate=True).then_inc(sem("nsa_max"), 1)
                    for a in range(2):
                        l, c = small[:, 32 + 8 * a:38 + 8 * a], small[:, 48 + 6 * a:54 + 6 * a]
                        dve.wait_ge(sem("nsa_exp"), 2 * i + (2 * n + a + 1))
                        link(v.reciprocal(l, l))
                        three = lambda ap: ap.rearrange("p (b r) -> p b r", r=NBR)
                        v.tensor_tensor(three(c), three(l), gtok[:, :, ds(i * NBR + NBR * (2 * n + GRP * a), NBR)], ALU.mult)\
                            .then_inc(sem("nsa_coef"), 1)
                        if before:
                            taps(i + (n - 1), *((0, 8) if a == 0 else (8, TAPS)))
                    used(ph, i, 4)
                    take(glu[:, 0, :], 0)
                    take(glu[:, 1, :], 1)
                    dve.wait_ge(sem("nsa_pv"), i + (n + 1))
                    y = tile(yp, i + n)
                    link(v.tensor_copy(y[:, 0:T], banks[:, 4, 0:T]))
                    v.tensor_tensor(y[:, T:], banks[:, 4, 0:T], y[:, 0:T].bitcast(f32), ALU.subtract).then_inc(sem("nsa_out"), 1)
                    dve.wait_ge(sem("glu_exp"), i + (n + 1))
                    link(v.tensor_scalar(glu[:, 1, :], glu[:, 1, :], 1.0, None, ALU.add))
                    link(v.reciprocal(glu[:, 1, :], glu[:, 1, :]))
                    link(v.tensor_tensor(uc[:, 32:], glu[:, 0, :], glu[:, 1, :], ALU.mult))
                    if last and pr == 1:
                        taps(GRP * 2 - 1, 0, TAPS)
                        first("w_out")

                if pr == 0:
                    step(0, False, before=False)
                loop(ph, step, 1 - pr)

            def taps(e, k0, k1):
                sums = (tile(conv_y, e), glu[:, 0, :])
                for k in range(k0, k1):
                    acc, u = sums[k % 2], uc[:, 32 - (TAPS - 1) + k:32 - (TAPS - 1) + k + T]
                    w = vdyn("conv_w", e + k * CT)
                    if k == 0:
                        ins = v.tensor_scalar(acc, u, w, vdyn("conv_b", e), ALU.mult, ALU.add)
                    elif k == 1:
                        ins = v.tensor_scalar(acc, u, w, None, ALU.mult)
                    else:
                        ins = v.scalar_tensor_tensor(acc, u, w, acc, ALU.mult, ALU.add)
                    if k % 2 or k == TAPS - 1:
                        link(ins)
                if k1 == TAPS:
                    link(v.tensor_tensor(sums[0], sums[0], sums[1], ALU.add))

            nsa(0)
            nsa(1)
            v.memset(small[:, 6:7], 0.0).then_inc(sem("conv_done"), 1)
            dve.wait_ge(sem("conv_sum"), 1)
            link(v.tensor_scalar(nv[:, 0, :], banks[:, 4, 0:T], 1.0 / CCH, None, ALU.mult))
            v.tensor_tensor(conv_y, conv_y, bcast(nv[:, 0, :], CT), ALU.subtract).then_inc(sem("conv_centred"), 1)
            dve.wait_ge(sem("conv_sum"), 2)
            root_of(banks[:, 5, 0:T], CCH, ROOT["conv"])
            link(v.tensor_tensor(conv_y, conv_y, bcast(nv[:, 2, :], CT), ALU.mult))
            for t in range(CT):
                ins = v.tensor_scalar(conv_y[:, t, :], conv_y[:, t, :], vcol("conv_ln_g", t), vcol("conv_ln_b", t), ALU.mult, ALU.add)
            ins.then_inc(sem("conv_affine"), 1)
            dve.wait_ge(sem("conv_sigmoid"), 1)
            v.tensor_tensor(conv_y, conv_y, sq[:, 0:CT, :], ALU.mult).then_inc(sem("conv_gated"), 1)
            dve.wait_ge(sem("conv_hi"), 1)
            v.tensor_tensor(yp[:, CT:KT, T:], conv_y, yp[:, CT:KT, 0:T].bitcast(f32), ALU.subtract).then_inc(sem("mixed"), 1)

            def residual(c0):
                def run(i):
                    for c in range(c0, c0 + 2):
                        xt = tile(x, i * 4 + c)
                        link(v.tensor_tensor(xt, banks[:, c, 0:T], xt, ALU.add))
                        v.tensor_tensor(xt, banks[:, c, T:], xt, ALU.add).then_inc(chunk_out, 1)
                return run

            stream("w_out", residual(0), residual(2))
            norm(1)

            def ffn(blk):
                if blk == 1:
                    v.memset(ua[:, :, 0:FTAPS - 1], 0.0)
                    link(v.memset(ug[:, :, 0:FTAPS - 1], 0.0))
                for p, (t0, n) in enumerate(PARTS):
                    up, down = f"up{blk}_{p}", f"down{blk}_{p}"
                    done = (blk - 1) * FT // 2 + t0 // 2

                    def conv(i, b0, buf, dst, ch0, name=None):
                        for c in range(2):
                            take(buf[:, c, FTAPS - 1:], b0 + c)
                        at_ch = [i * 2 + (ch0 + t0 + c) for c in range(2)]
                        at.wait_for(chunk_out, i * 4 + (C0[up] + b0 + 2 + LEAD))
                        for c in range(2):
                            ins = v.tensor_scalar(dst[:, c, :], buf[:, c, FTAPS - 1:],
                                                  vdyn("ffn_conv_w", at_ch[c] + (FTAPS - 1) * 2 * FT),
                                                  vdyn("ffn_conv_b", at_ch[c]), ALU.mult, ALU.add)
                        link(ins)
                        for k in range(FTAPS - 2, -1, -1):
                            for c in range(2):
                                ins = v.scalar_tensor_tensor(dst[:, c, :], buf[:, c, k:k + T],
                                                             vdyn("ffn_conv_w", at_ch[c] + k * 2 * FT), dst[:, c, :],
                                                             ALU.mult, ALU.add)
                            if k:
                                link(ins)
                        if name:
                            ins.then_inc(sem(name), 1)
                        else:
                            link(ins)

                    def out_a(i):
                        if blk == 1:
                            conv(i, 0, ua, ca, 0)
                        else:
                            for c in range(2):
                                take(ca[:, c, :], c)

                    def out_b(i):
                        if blk == 1:
                            conv(i, 2, ug, cg, FT, "ffn_gate")
                        else:
                            take(cg[:, 0, :], 2)
                            take(cg[:, 1, :], 3)
                            at.wait_for(chunk_out, i * 4 + (C0[up] + 4 + LEAD))
                            v.memset(small[:, 7:8], 0.0).then_inc(sem("ffn_gate"), 1)

                    def work(i):
                        dve.wait_ge(sem("ffn_sigmoid"), i + (done + 1))
                        link(v.tensor_tensor(sg, sg, cg, ALU.mult))
                        link(v.tensor_tensor(ca, ca, sg, ALU.mult))
                        mid = yp[:, ds(i * 2, 2), :]
                        link(v.tensor_copy(mid[:, :, 0:T], ca))
                        v.tensor_tensor(mid[:, :, T:], ca, mid[:, :, 0:T].bitcast(f32), ALU.subtract).then_inc(sem("mid"), 1)
                        at.wait_for(sem("mid"), i + (done + 1))

                    stream(up, out_a, out_b, work)
                    stream(down, residual(0), residual(2), pre_next=not (blk == 2 and p == 2))

            ffn(1)
            norm(2)
            norm(3)

            stream("latent", to(lat, 0), to(lat, 2))
            used("latent_last", 0, 4)
            for c in range(2):
                take(lat[:, 8 + c, :], c)
            used("kpe", 0, 2)
            take(kraw, 2)

            def rope(dst, raw, src):
                link(v.tensor_tensor(dst, raw, c_("cos"), ALU.mult))
                link(v.tensor_tensor(raw, src, c_("sin"), ALU.mult))
                return v.tensor_tensor(dst, dst, raw, ALU.add)

            dve.wait_ge(sem("kpe_turned"), 1)
            link(rope(kpe, kraw, banks[:, 6, 0:T]))
            for k, (name, a, b, n) in enumerate((("q_norm_g_2", 0, QT, RQ), ("kv_norm_g_2", QT, QT + KVT, RKV))):
                dve.wait_ge(sem("latent_sum"), k + 1)
                root_of(banks[:, 4 + k, 0:T], n, ROOT["latent"] + k)
                for t in range(a, b):
                    ins = v.scalar_tensor_tensor(lat[:, t, :], lat[:, t, :], vcol(name, t - a), nv[:, 2, :], ALU.mult, ALU.mult)
                link(ins)
                link(v.tensor_copy(yp[:, a:b, 0:T], lat[:, a:b, :]))
                v.tensor_tensor(yp[:, a:b, T:], lat[:, a:b, :], yp[:, a:b, 0:T].bitcast(f32), ALU.subtract).then_inc(sem("latent_pair"), 1)
            dve.wait_ge(sem("lambda_mm"), 1)
            v.tensor_copy(small[:, 2:4], banks[:, 7, 0:2]).then_inc(sem("lambda_sums"), 1)
            dve.wait_ge(sem("lambda_exp"), 1)
            link(v.tensor_tensor(small[:, 6:7], small[:, 5:6], small[:, 4:5], ALU.subtract))
            link(v.tensor_scalar(small[:, 6:7], small[:, 6:7], -LAM0, None, ALU.add))

            def maxima(a, scale, name):
                m = small[:, 16 + 2 * a:18 + 2 * a]
                v.tensor_reduce(m[:, 0:1], S2[:, a, 0:P], X, ALU.max, negate=True)
                link(v.tensor_reduce(m[:, 1:2], S2[:, a, P:], X, ALU.max, negate=True))
                v.tensor_scalar(m, m, scale, None, ALU.mult).then_inc(sem(name), 1)

            def gate_done(i, dst, c0):
                dve.wait_ge(sem("bgate_exp"), i + (c0 + 1))
                link(v.tensor_scalar(gt, gt, 1.0, None, ALU.add))
                return v.reciprocal(dst[:, ds(i * 2, 2), :], gt)

            def mla(i, last):
                ph = "mla"
                used(ph, i, 2)
                take(qn[:, 0, :], 0)
                take(qn[:, 1, :], 1)
                take(qraw, 2)
                used(ph, i, 3)
                take(kn[:, 0, :], 3)
                take(vf[:, 0, :], 0)
                dve.wait_ge(sem("mla_rot"), i + 1)
                rope(qr, qraw, banks[:, 7, 0:T]).then_inc(sem("mla_q"), 1)
                used(ph, i, 4)
                take(kn[:, 1, :], 1)
                take(vf[:, 1, :], 2)
                dve.wait_ge(sem("mla_vturned"), i + 1)
                v.tensor_copy(vt2, banks[:, 6, :].rearrange("p (a n) -> p a n", a=4)).then_inc(sem("mla_v"), 1)
                for a in range(2):
                    dve.wait_ge(sem("mla_scores"), 2 * i + (a + 1))
                    link(v.tensor_tensor(S2[:, a, :], banks[:, 4 + a, 0:3 * P], c_("mask"), ALU.add))
                    maxima(a, MSCALE, "mla_max")
                for a in range(2):
                    dve.wait_ge(sem("mla_exp"), 2 * i + (a + 1))
                    l = small[:, 24 + 2 * a:26 + 2 * a]
                    link(v.reciprocal(l, l))
                    v.tensor_scalar(S2[:, a, 0:P], S2[:, a, 0:P], l[:, 0:1], None, ALU.mult)
                    v.tensor_scalar(S2[:, a, P:], S2[:, a, P:], l[:, 1:2], None, ALU.mult).then_inc(sem("mla_p"), 1)
                used(ph, i, 8)
                take(gt[:, 0, :], 3)
                take(gt[:, 1, :], 0)
                for a in range(2):
                    dve.wait_ge(sem("mla_turned"), 2 * i + (a + 1))
                    v.tensor_copy(pt2[:, a, :], banks[:, 6 if a == 0 else 4, 0:3 * P]).then_inc(sem("mla_pt"), 1)
                dve.wait_ge(sem("mla_pv"), i + 1)
                v.tensor_copy(y_f[:, ds(i * 2, 2), :], banks[:, 7, :].rearrange("p (a n) -> p a n", a=2)).then_inc(sem("mla_out"), 1)
                link(gate_done(i, merged, 0))
                if last:
                    first(FIRST[ph])

            loop("mla", mla)
            for b in range(4):
                dve.wait_ge(sem("mla_hi"), b + 1)
                v.tensor_tensor(yp[:, 4 * b:4 * b + 4, T:], y_f[:, 4 * b:4 * b + 4, :],
                                yp[:, 4 * b:4 * b + 4, 0:T].bitcast(f32), ALU.subtract).then_inc(sem("mla_lo"), 1)

            def project(ph, c0):
                def run(i):
                    for c in range(c0, c0 + 2):
                        take(tmp[:, c, :], c)
                    at.wait_for(chunk_out, i * 4 + (C0[ph] + c0 + 2 + LEAD))
                    if ph == "diff_proj":
                        for c in range(c0, c0 + 2):
                            ins = v.tensor_tensor(tmp[:, c, :], tmp[:, c, :], tile(gate2, i * 4 + c), ALU.mult)
                        link(ins)
                    for c in range(c0, c0 + 2):
                        m = tile(merged, i * 4 + c)
                        ins = v.tensor_tensor(m, m, tmp[:, c, :], ALU.add if ph == "diff_proj" else ALU.mult)
                    link(ins)
                return run

            stream("mla_proj", project("mla_proj", 0), project("mla_proj", 2))

            def diff(i, last):
                ph = "diff"
                used(ph, i, 4)
                take(dq[:, 0, :], 0)
                take(dq[:, 1, :], 1)
                used(ph, i, 8)
                take(dk[:, 0, :], 2)
                take(dk[:, 1, :], 3)
                for a in range(2):
                    dve.wait_ge(sem("diff_scores"), 2 * i + (a + 1))
                    link(v.scalar_tensor_tensor(S2[:, a, :], c_("dist"), cst[:, ds(i + CST["slope"][0], 1)],
                                                banks[:, 4 + a, 0:3 * P], ALU.mult, ALU.add))
                    maxima(a, DSCALE, "diff_max")
                dve.wait_ge(sem("diff_exp"), 2 * i + 2)
                l = small[:, 24:28]
                link(v.reciprocal(l, l))
                link(v.tensor_scalar(l[:, 2:4], l[:, 2:4], small[:, 6:7], None, ALU.mult))
                for b, (lo_, hi_) in enumerate(((0, P), (P, 3 * P))):
                    ins = v.tensor_scalar(S2[:, 0, lo_:hi_], S2[:, 0, lo_:hi_], l[:, b:b + 1], None, ALU.mult)
                link(ins)
                for b, (lo_, hi_) in enumerate(((0, P), (P, 3 * P))):
                    ins = v.scalar_tensor_tensor(S2[:, 0, lo_:hi_], S2[:, 1, lo_:hi_], l[:, 2 + b:3 + b], S2[:, 0, lo_:hi_],
                                                 ALU.mult, ALU.add)
                ins.then_inc(sem("diff_p"), 1)
                used(ph, i, 12)
                take(vf[:, 0, :], 0)
                take(vf[:, 1, :], 1)
                dve.wait_ge(sem("diff_vturned"), i + 1)
                v.tensor_copy(vt2, banks[:, 6, :].rearrange("p (a n) -> p a n", a=4)).then_inc(sem("diff_v"), 1)
                used(ph, i, 16)
                take(gt[:, 0, :], 2)
                take(gt[:, 1, :], 3)
                dve.wait_ge(sem("diff_turned"), i + 1)
                v.tensor_copy(pt2[:, 0, :], banks[:, 4, 0:3 * P]).then_inc(sem("diff_pt"), 1)
                dve.wait_ge(sem("diff_pv"), i + 1)
                v.tensor_copy(o_sb, banks[:, 7, :].rearrange("p (a n) -> p a n", a=2)).then_inc(sem("o_out"), 1)
                link(gate_done(i, gate2, STEPS["mla"]))
                dve.wait_ge(sem("o_sum"), i + 1)
                root_of(banks[:, 5, 0:T], 2 * P, i + ROOT["heads"])
                for c in range(2):
                    ins = v.scalar_tensor_tensor(o_sb[:, c, :], o_sb[:, c, :], vcol("diff_norm_g_2", c), nv[:, 2, :], ALU.mult, ALU.mult)
                link(ins)
                y = yp[:, ds(i * 2, 2), :]
                link(v.tensor_copy(y[:, :, 0:T], o_sb))
                v.tensor_tensor(y[:, :, T:], o_sb, y[:, :, 0:T].bitcast(f32), ALU.subtract).then_inc(sem("diff_mixed"), 1)
                if last:
                    first(FIRST[ph])

            loop("diff", diff)

            def split_merged(i):
                m, h = merged[:, ds(i * 4, 4), :], hp[:, ds(i * 4, 4), :]
                link(v.tensor_copy(h[:, :, 0:T], m))
                v.tensor_tensor(h[:, :, T:], m, h[:, :, 0:T].bitcast(f32), ALU.subtract).then_inc(sem("merged_lo"), 1)

            stream("diff_proj", project("diff_proj", 0), project("diff_proj", 2), split_merged)
            stream("w_out_2", residual(0), residual(2))
            norm(4)
            ffn(2)
            norm(5)
            for k in range(8):
                dve.wait_ge(sem("out_turned"), k + 1)
                v.tensor_copy(out_tok[:, k // 4, (k % 4) * 512:(k % 4 + 1) * 512], banks[:, k, :]).then_inc(sem("out_ready"), 1)

        @block.tensor
        def _(pe):
            mm = nc.tensor.matmul

            def turn(dst, src, rows=P):
                return nc.tensor.transpose(dst, src, ident[0:rows, 0:rows])

            def unit(ph, i, j, k0, ku, cols, where, rhs, kt_last, operand=None):
                s, r = slot_of(ph, j)
                if operand:
                    pe.wait_ge(*operand)
                pe.wait_ge(lo_ready[s], i * (UPS[ph] // R) + (r + 2))
                for k in range(ku):
                    kt = k0 + k
                    for c, b in enumerate(where):
                        at = k * cols + c * P
                        mm(banks[:, b, :], w_hi[:, s, at:at + P], rhs[:, kt, :], start=kt == 0, stop=False)
                        ins = mm(banks[:, b, 0:T], w_lo[:, s, at:at + P], rhs[:, kt, 0:T], start=False, stop=kt == kt_last)
                ins.then_inc(unit_used, 1)

            def free(ph, i, chunks):
                pe.wait_ge(chunk_out, i * CPS[ph] + (C0[ph] + chunks + LEAD))

            def gemm(ph, rhs, ktiles, operand, k_norm=None, between=None, whole_before=False):
                if whole_before:
                    free(ph, 0, 0)
                ku = ktiles // 4

                def step(i, last):
                    for g in range(2):
                        if last and g == 1:
                            norm(k_norm, 0, KT - 4)
                        free(ph, i, -2 + 2 * g)
                        for u in range(4):
                            if between and isinstance(i, int) and i == 0 and (g, u) == (0, 2):
                                between()
                            unit(ph, i, 4 * g + u, u * ku, ku, GC, (2 * g, 2 * g + 1), rhs, ktiles - 1, operand(u))

                whole = STEPS[ph] - (k_norm is not None)
                if between:
                    step(0, False)
                with pe.Fori(1 if between else 0, whole) as i:
                    step(i, False)
                if k_norm is not None:
                    step(whole, True)
                    norm(k_norm, KT - 4, KT)

            def sums(dst, src, n):
                for t in range(n):
                    ins = mm(dst, ones, src[:, t, :], start=t == 0, stop=t == n - 1)
                return ins

            def norm(k, t0=0, t1=KT):
                for t in range(t0, t1):
                    if t % 2 == 0:
                        pe.wait_ge(sem("squares"), KT // 2 * k + t // 2 + 1)
                    ins = mm(banks[:, 4, 0:T], ones, sq[:, t, :], start=t == 0, stop=t == KT - 1)
                if t1 == KT:
                    ins.then_inc(sem("sum_of_squares"), 1)

            pe.wait_ge(loaded["cst"], 16)
            pe.wait_ge(loaded["bias_rows"], 16)
            mm(banks[0:NQ, 7, 0:T], small[0:NBKT, 0:NQ], c_("onehot", NBKT, 0, T), start=True, stop=True).then_inc(sem("bias_mm"), 1)
            pe.wait_ge(loaded["x"], 16)
            for k in range(8):
                if k == 7:
                    pe.wait_ge(sem("bias_row"), 1)
                for t in range(2):
                    for b in range(QB):
                        ins = turn(banks[:, k, t * T + b * P:t * T + (b + 1) * P], x_tok[:, b, (2 * k + t) * P:(2 * k + t + 1) * P])
                ins.then_inc(sem("x_turned"), 1)
            pe.wait_ge(loaded["vec"], 16 * VEC_LOADS)
            pe.wait_ge(sem("x_transposed"), 2)
            for t in range(VT):
                ins = turn(banks[:, t // 4, (t % 4) * P:(t % 4 + 1) * P], vec_rows[:, t, :])
                if t == 3:
                    ins.then_inc(unit_used, LEAD)
            ins.then_inc(sem("vec_turned"), 1)
            pe.wait_ge(sem("x_transposed"), 8)
            norm(0)

            def normed(k):
                return lambda u: (sem("normed_lo"), 4 * NSPLIT[k] + u + 1)

            gemm("q", hp, KT, normed(0), whole_before=True)
            gemm("kv", hp, KT, normed(0))
            free("gates", 0, 0)
            for u in range(2):
                unit("gates", 0, u, 8 * u, 8, P, (0,), hp, KT - 1)
            pe.wait_ge(chunk_out, C0["gates"] + LEAD)
            for k in range(QB):
                for a in range(2):
                    ins = turn(banks[:, 7, (2 * k + a) * P:(2 * k + a + 1) * P], kvT[:, 1, 1, a, k * P:(k + 1) * P])
            ins.then_inc(sem("v_turned"), 1)
            pe.wait_ge(loaded["cmp"], 16 * 12)
            for kv in range(2):
                ins = turn(banks[:, 5, kv * CLEN:(kv + 1) * CLEN], pos_rows[0:CLEN, kv].rearrange("p a d -> p (a d)"), CLEN)
            ins.then_inc(sem("pos_turned"), 1)
            free("gates", 0, 1)
            for b in range(QB):
                ins = turn(banks[:, 4, b * NBR * NQ:(b + 1) * NBR * NQ], g_sb[0:NBR * NQ, b * P:(b + 1) * P], NBR * NQ)
            ins.then_inc(sem("gates_turned"), 1)
            for kv, w1 in enumerate((w1k, w1v)):
                pe.wait_ge(sem("blocks"), kv + 1)
                for l in range(CLEN):
                    o, r = divmod(l, CSTR)
                    for a in range(2):
                        h = slice(a * HD, (a + 1) * HD)
                        blk = Xc[h, o].rearrange("p (a n) r -> p a n r", a=2)[:, :, o:o + NCMP, r]
                        ins = mm(banks[h, 6, 32 * kv:32 * kv + 2 * NCMP].rearrange("p (a n) -> p a n", a=2), w1[h, l, :], blk,
                                 start=l == 0, stop=l == CLEN - 1, skip_group_check=True)
                ins.then_inc(sem("hidden_mm"), 1)
            pe.wait_ge(sem("gates_tok"), 1)
            for k in range(QB):
                for a in range(2):
                    ins = turn(banks[:, 4, (2 * k + a) * P:(2 * k + a + 1) * P], kvT[:, 2, 1, a, k * P:(k + 1) * P])
            ins.then_inc(sem("v_turned"), 1)
            pe.wait_ge(sem("hidden_act"), 1)
            for a in range(2):
                h = slice(a * HD, (a + 1) * HD)
                mm(banks[h, 5, 128:128 + 2 * NCMP], w2[h, 0, :], hid[h, 0, 0, 0:2 * NCMP], start=True, stop=True)
                for pr in range(2):
                    c = 256 + pr * HD
                    ins = mm(banks[0:NCMP, 5 + a, c:c + HD], hid[h, 0, 1, pr * NCMP:(pr + 1) * NCMP], w2[h, 1, :], start=True, stop=True)
            ins.then_inc(sem("cmp_mm"), 1)
            pe.wait_ge(loaded["bias"], 16)
            pe.wait_ge(sem("v_tok"), 2)
            pe.wait_ge(sem("cmp_kv"), 1)
            for k in range(8):
                if k >= 2:
                    pe.wait_ge(sem("bias_ready"), k - 1)
                mm(banks[:, 6 + k % 2, :], c_("flip"), bias_win[:, 2 * k:2 * k + 2, :], start=True, stop=True).then_inc(sem("bias_flipped"), 1)
            pe.wait_ge(sem("bias_ready"), 8)
            pe.wait_ge(sem("cmp_kv"), 1)

            def nsa(pr):
                ph, n = f"conv{pr}", pr * GRP
                with pe.Fori(0, GRP) as i:
                    pe.wait_ge(sem("nsa_q"), i + (n + 1))
                    pe.wait_ge(sem("nsa_out"), i + (n + 1))
                    for a in range(2):
                        h = slice(a * HD, (a + 1) * HD)
                        q0, q1 = q_st[h, 0:P], q_st[h, P:T]
                        for br in range(2):
                            mm(banks[:, 4 + 2 * a, br * T:(br + 1) * T], q1, kvT[h, 1 + br, 0, pr, :], start=True, stop=True)
                            mm(banks[:, 5 + 2 * a, br * P:(br + 1) * P], q0, kvT[h, 1 + br, 0, pr, 0:P], start=True, stop=True)
                        kc = kcm[h, pr * NCMP:(pr + 1) * NCMP]
                        mm(banks[:, 5 + 2 * a, 256:256 + NCMP], q1, kc, start=True, stop=True)
                        mm(banks[:, 5 + 2 * a, 272:272 + NCMP0], q0, kc[:, 0:NCMP0], start=True, stop=True).then_inc(sem("nsa_scores"), 1)
                    free(ph, i, 0)
                    for u in range(4):
                        unit(ph, i, u, 4 * u, 4, GC, (0, 1), hp, KT - 1)
                    for a in range(2):
                        e = S[a]
                        pe.wait_ge(sem("nsa_p"), 2 * i + (2 * n + a + 1))
                        for c, lo_ in enumerate((512, 0, 640, 256)):
                            turn(banks[:, 4 + 2 * a, c * P:(c + 1) * P], e[:, lo_:lo_ + P])
                        for c, lo_ in enumerate((128, 384)):
                            turn(banks[:, 5 + 2 * a, c * P:(c + 1) * P], e[:, lo_:lo_ + P])
                        turn(banks[0:NCMP0, 5 + 2 * a, 256:384], e[:, 784:784 + NCMP0])
                        turn(banks[0:NCMP, 5 + 2 * a, 384:512], e[:, 768:768 + NCMP]).then_inc(sem("nsa_turned"), 1)
                    for a in range(2):
                        h = slice(a * HD, (a + 1) * HD)
                        pe.wait_ge(sem("nsa_pt"), 2 * i + (2 * n + a + 1))
                        o = banks[h, 4, 0:T]
                        mm(o, vtm[:, 0, 0, pr, h], ptA[a][:, 0:T], start=True, stop=False)
                        mm(o, vtm[:, 1, 0, pr, h], ptA[a][:, T:2 * T], start=False, stop=False)
                        mm(o[:, P:T], vtm[:, 0, 1, pr, h], ptB[a][:, 0:P], start=False, stop=False)
                        mm(o[:, P:T], vtm[:, 1, 1, pr, h], ptB[a][:, P:T], start=False, stop=False)
                        mm(o[:, 0:P], vcm[0:NCMP0, pr, h], ptB[a][0:NCMP0, 256:384], start=False, stop=False)
                        ins = mm(o[:, P:T], vcm[0:NCMP, pr, h], ptB[a][0:NCMP, 384:512], start=False, stop=True)
                    ins.then_inc(sem("nsa_pv"), 1)

            nsa(0)
            nsa(1)

            def conv_sums():
                pe.wait_ge(sem("conv_done"), 1)
                sums(banks[:, 4, 0:T], conv_y, CT).then_inc(sem("conv_sum"), 1)
                pe.wait_ge(sem("conv_squares"), 1)
                sums(banks[:, 5, 0:T], sq, CT).then_inc(sem("conv_sum"), 1)

            gemm("w_out", yp, KT, lambda u: (sem("mixed"), 1) if u >= 2 else (sem("nsa_out"), 2 * GRP + 1), 1,
                 between=conv_sums, whole_before=True)

            def ffn(blk, k):
                for p, (t0, n) in enumerate(PARTS):
                    gemm(f"up{blk}_{p}", hp, KT, normed(k))
                    done = (blk - 1) * FT // 2 + t0 // 2
                    gemm(f"down{blk}_{p}", yp, n, lambda u: (sem("mid"), done + -(-(u + 1) * (n // 4) // 2)),
                         3 * blk - 1 if p == 2 else None)

            ffn(1, 1)
            norm(3)
            gemm("latent", hp, KT, normed(3))
            free("latent_last", 0, 0)
            for u in range(4):
                unit("latent_last", 0, u, 4 * u, 4, GC, (0, 1), hp, KT - 1)
            for u in range(2):
                unit("kpe", 0, u, 8 * u, 8, P, (2,), hp, KT - 1)
            pe.wait_ge(sem("latent_squares"), 1)
            sums(banks[:, 4, 0:T], latsq, QT).then_inc(sem("latent_sum"), 1)
            free("kpe", 0, 1)
            mm(banks[:, 6, 0:T], c_("rot"), kraw, start=True, stop=True).then_inc(sem("kpe_turned"), 1)
            pe.wait_ge(sem("latent_squares"), 2)
            sums(banks[:, 5, 0:T], latsq[:, QT:QT + KVT, :], KVT).then_inc(sem("latent_sum"), 1)
            mm(banks[:, 7, 0:2], ones, small[:, 8:10], start=True, stop=True).then_inc(sem("lambda_mm"), 1)

            free("mla", 0, 0)
            pe.wait_ge(sem("lambda_sums"), 1)
            with pe.Fori(0, STEPS["mla"]) as i:
                ph = "mla"
                free(ph, i, 0)
                for u in range(2):
                    unit(ph, i, u, 3 * u, 3, 384, (0, 1, 2), yp, QT - 1, (sem("latent_pair"), 1))
                free(ph, i, 1)
                lat_kv = yp[:, QT:QT + KVT, :]
                unit(ph, i, 2, 0, 4, GC, (3, 0), lat_kv, KVT - 1, (sem("latent_pair"), 2))
                free(ph, i, 3)
                mm(banks[:, 7, 0:T], c_("rot"), qraw, start=True, stop=True).then_inc(sem("mla_rot"), 1)
                unit(ph, i, 3, 0, 4, GC, (1, 2), lat_kv, KVT - 1)
                pe.wait_ge(sem("mla_q"), i + 1)
                free(ph, i, 7)
                for a in range(2):
                    h = slice(a * ROPE, (a + 1) * ROPE)
                    for b in range(QB):
                        o = banks[:, 4 + a, b * P:b * P + (b + 1) * P]
                        mm(o, qn[:, a, b * P:(b + 1) * P], kn[:, a, 0:(b + 1) * P], start=True, stop=False)
                        ins = mm(o, qr[h, b * P:(b + 1) * P], kpe[h, 0:(b + 1) * P], start=False, stop=True)
                    ins.then_inc(sem("mla_scores"), 1)
                for a in range(2):
                    for k in range(QB):
                        ins = turn(banks[:, 6, (2 * a + k) * P:(2 * a + k + 1) * P], vf[:, a, k * P:(k + 1) * P])
                ins.then_inc(sem("mla_vturned"), 1)
                for u in range(4):
                    unit(ph, i, 4 + u, 4 * u, 4, GC, (3, 0), hp, KT - 1)
                pe.wait_ge(sem("mla_v"), i + 1)
                for a in range(2):
                    pe.wait_ge(sem("mla_p"), 2 * i + (a + 1))
                    for c in range(3):
                        ins = turn(banks[:, 6 if a == 0 else 4, c * P:(c + 1) * P], S2[:, a, c * P:(c + 1) * P])
                    ins.then_inc(sem("mla_turned"), 1)
                for a in range(2):
                    pe.wait_ge(sem("mla_pt"), 2 * i + (a + 1))
                    o = banks[:, 7, a * T:(a + 1) * T]
                    mm(o, vt2[:, 2 * a, :], pt2[:, a, 0:T], start=True, stop=False)
                    ins = mm(o[:, P:T], vt2[:, 2 * a + 1, :], pt2[:, a, T:3 * P], start=False, stop=True)
                ins.then_inc(sem("mla_pv"), 1)
            gemm("mla_proj", yp, KT, lambda u: (sem("mla_lo"), u + 1), whole_before=True)

            free("diff", 0, 0)
            with pe.Fori(0, STEPS["diff"]) as i:
                ph = "diff"

                def group(j, where):
                    for u in range(4):
                        unit(ph, i, 4 * j + u, 4 * u, 4, GC, where, hp, KT - 1)

                free(ph, i, -2)
                group(0, (0, 1))
                free(ph, i, 0)
                group(1, (2, 3))
                free(ph, i, 4)
                for a in range(2):
                    for b in range(QB):
                        ins = mm(banks[:, 4 + a, b * P:b * P + (b + 1) * P], dq[:, a, b * P:(b + 1) * P], dk[:, a, 0:(b + 1) * P],
                                 start=True, stop=True)
                    ins.then_inc(sem("diff_scores"), 1)
                group(2, (0, 1))
                group(3, (2, 3))
                free(ph, i, 6)
                for k in range(QB):
                    for c in range(2):
                        ins = turn(banks[:, 6, (2 * k + c) * P:(2 * k + c + 1) * P], vf[:, c, k * P:(k + 1) * P])
                ins.then_inc(sem("diff_vturned"), 1)
                pe.wait_ge(sem("diff_p"), i + 1)
                for c in range(3):
                    ins = turn(banks[:, 4, c * P:(c + 1) * P], S2[:, 0, c * P:(c + 1) * P])
                ins.then_inc(sem("diff_turned"), 1)
                pe.wait_ge(sem("diff_v"), i + 1)
                pe.wait_ge(sem("diff_pt"), i + 1)
                for c in range(2):
                    o = banks[:, 7, c * T:(c + 1) * T]
                    mm(o, vt2[:, c, :], pt2[:, 0, 0:T], start=True, stop=False)
                    ins = mm(o[:, P:T], vt2[:, 2 + c, :], pt2[:, 0, T:3 * P], start=False, stop=True)
                ins.then_inc(sem("diff_pv"), 1)
                pe.wait_ge(sem("o_squares"), i + 1)
                sums(banks[:, 5, 0:T], o_sq, 2).then_inc(sem("o_sum"), 1)
            gemm("diff_proj", yp, KT, lambda u: (sem("diff_mixed"), 2 * (u + 1)), whole_before=True)
            gemm("w_out_2", hp, KT, lambda u: (sem("merged_lo"), u + 1), 4)
            ffn(2, 4)
            for k in range(8):
                b, q = divmod(k, 4)
                pe.wait_ge(sem("final_normed"), q + 1)
                for c in range(4):
                    ins = turn(banks[:, k, c * P:(c + 1) * P], nrm[:, 4 * q + c, b * P:(b + 1) * P])
                ins.then_inc(sem("out_turned"), 1)


_INS = ["x", "rel_bias", "mix_norm_g", "w_in", "cmp_pos", "cmp_w1", "cmp_w2", "conv_w", "conv_b", "conv_ln_g", "conv_ln_b",
        "w_out", "ffn_norm_g", "w_up", "ffn_conv_w", "ffn_conv_b", "w_down", "final_norm_g", "attn_norm_g_2", "w_in_2",
        "b_gate_2", "q_norm_g_2", "w_uq_2", "kv_norm_g_2", "w_ukv_2", "lambda_q1_2", "lambda_k1_2", "lambda_q2_2",
        "lambda_k2_2", "diff_norm_g_2", "w_mla_proj_2", "w_diff_proj_2", "w_out_2", "ffn_norm_g_2", "w_ffn_gate_2",
        "w_ffn_up_2", "w_ffn_down_2", "final_norm_g_2"]


def kernel(**inputs):
    import numpy as _np
    import concourse.bacc as _bacc
    from concourse import mybir as _mybir
    from concourse.bass_utils import run_bass_kernel_spmd as _run

    nc = _bacc.Bacc("TRN2", target_bir_lowering=False, num_devices=1)
    arrays, aps = {}, {}
    for name in _INS:
        a = _np.ascontiguousarray(inputs[name])
        arrays[f"in_{name}"] = a
        aps[name] = nc.dram_tensor(f"in_{name}", a.shape, _mybir.dt.from_np(a.dtype), kind="ExternalInput").ap()
    arrays["tables"] = constants()
    cst = nc.dram_tensor("tables", (P, NCST), _mybir.dt.float32, kind="ExternalInput").ap()
    out = nc.dram_tensor("out", (1, T, D), _mybir.dt.float32, kind="ExternalOutput").ap()
    program(nc, aps, cst, out)
    r = _run(nc, [arrays], core_ids=[0])
    return r.results[0]["out"]
```
